# Optimizing a Trainium2 kernel written in Bass

```python
import math
import jax, jax.numpy as jnp
from jax import lax
import numpy as np

D_MODEL = 1024
BATCH = 1
SEQ = 256
DEPTH = 2

N_A_LAYERS = DEPTH // 2
N_B_LAYERS = DEPTH - N_A_LAYERS

DN_HEADS = 8
DN_HEAD_DIM = D_MODEL // DN_HEADS
DN_WIDTH = DN_HEADS * DN_HEAD_DIM
CONV_K = 4
DN_CHUNK = 64

DA_HEADS = 8
DA_HEAD_DIM = D_MODEL // (2 * DA_HEADS)
DA_V_DIM = 2 * DA_HEAD_DIM
DA_QK_WIDTH = 2 * DA_HEADS * DA_HEAD_DIM
DA_WIDTH = DA_HEADS * DA_V_DIM
Q_BLOCK = 128

N_GROUPS = 4
EXPERTS_PER_GROUP = 8
N_EXPERTS = N_GROUPS * EXPERTS_PER_GROUP
TOP_K = 2
EXPERT_FF = D_MODEL // 2
MOE_BLOCK = 128

ALPHA = (2 * DEPTH) ** 0.25
BETA_INIT = (8 * DEPTH) ** -0.25
LN_EPS = 1e-5
RMS_EPS = 1e-6


def layer_norm(x, g, b):
    xf = x.astype(jnp.float32)
    mu = jnp.mean(xf, axis=-1, keepdims=True)
    var = jnp.mean(jnp.square(xf - mu), axis=-1, keepdims=True)
    return ((xf - mu) * lax.rsqrt(var + LN_EPS) * g + b).astype(x.dtype)

def rms_norm(x, w):
    xf = x.astype(jnp.float32)
    return xf * lax.rsqrt(jnp.mean(jnp.square(xf), axis=-1, keepdims=True) + RMS_EPS) * w.astype(jnp.float32)

def l2_normalize(x):
    xf = x.astype(jnp.float32)
    return xf * lax.rsqrt(jnp.sum(jnp.square(xf), axis=-1, keepdims=True) + RMS_EPS)

def causal_depthwise_conv(x, w):
    k_width, t = w.shape[0], x.shape[1]
    xp = jnp.pad(x, ((0, 0), (k_width - 1, 0), (0, 0)))
    y = xp[:, 0:t] * w[0]
    for j in range(1, k_width):
        y = y + xp[:, j:j + t] * w[j]
    return y

def chunked_gated_delta_rule(q, k, v, g, beta):
    b, t, h, dk = q.shape
    dv = v.shape[-1]
    n, c = t // DN_CHUNK, DN_CHUNK

    def to_chunks(a):
        return jnp.moveaxis(a.reshape((b, n, c, h) + a.shape[3:]), 3, 1)

    q = to_chunks(q * dk ** -0.5)
    k = to_chunks(k)
    v = to_chunks(v.astype(jnp.float32))
    gc = jnp.cumsum(to_chunks(g), axis=-1)
    beta = to_chunks(beta)
    idx = jnp.arange(c)
    causal = idx[:, None] >= idx[None, :]
    strict = idx[:, None] > idx[None, :]
    decay = jnp.exp(jnp.where(causal, gc[..., :, None] - gc[..., None, :], -jnp.inf))
    k_beta = k * beta[..., None]
    a_mat = jnp.where(strict, jnp.einsum('bhnid,bhnjd->bhnij', k_beta, k) * decay, 0.0)
    rhs = jnp.concatenate([v * beta[..., None], k_beta * jnp.exp(gc)[..., None]], axis=-1)
    sol = lax.linalg.triangular_solve(a_mat + jnp.eye(c, dtype=jnp.float32), rhs,
                                      left_side=True, lower=True, unit_diagonal=True)
    u, w = sol[..., :dv], sol[..., dv:]
    attn = jnp.where(causal, jnp.einsum('bhnid,bhnjd->bhnij', q, k) * decay, 0.0)
    q_dec = q * jnp.exp(gc)[..., None]
    k_dec = k * jnp.exp(gc[..., -1:] - gc)[..., None]
    g_last = jnp.exp(gc[..., -1])

    def step(state, xs):
        u_i, w_i, q_i, k_i, attn_i, gl_i = xs
        v_new = u_i - jnp.einsum('bhcd,bhdv->bhcv', w_i, state)
        o_i = jnp.einsum('bhcd,bhdv->bhcv', q_i, state) + jnp.einsum('bhij,bhjv->bhiv', attn_i, v_new)
        state = state * gl_i[..., None, None] + jnp.einsum('bhcd,bhcv->bhdv', k_i, v_new)
        return state, o_i

    xs = tuple(jnp.moveaxis(a, 2, 0) for a in (u, w, q_dec, k_dec, attn, g_last))
    state0 = jnp.zeros((b, h, dk, dv), jnp.float32)
    _, o = lax.scan(step, state0, xs)
    return o.transpose(1, 0, 3, 2, 4).reshape(b, t, h, dv)

def gated_deltanet(x, w_in, conv_w, a_log, dt_bias, norm_w, w_out):
    b, t, _ = x.shape
    proj = x @ w_in
    qkv = jax.nn.silu(causal_depthwise_conv(proj[..., :3 * DN_WIDTH], conv_w))
    qkv = qkv.reshape(b, t, 3, DN_HEADS, DN_HEAD_DIM)
    q = l2_normalize(qkv[:, :, 0])
    k = l2_normalize(qkv[:, :, 1])
    v = qkv[:, :, 2]
    z = proj[..., 3 * DN_WIDTH:4 * DN_WIDTH].reshape(b, t, DN_HEADS, DN_HEAD_DIM)
    beta = jax.nn.sigmoid(proj[..., 4 * DN_WIDTH:4 * DN_WIDTH + DN_HEADS].astype(jnp.float32))
    alpha_logit = proj[..., 4 * DN_WIDTH + DN_HEADS:].astype(jnp.float32)
    g = -jnp.exp(a_log.astype(jnp.float32)) * jax.nn.softplus(alpha_logit + dt_bias.astype(jnp.float32))
    o = chunked_gated_delta_rule(q, k, v, g, beta)
    o = rms_norm(o, norm_w) * jax.nn.silu(z.astype(jnp.float32))
    return o.reshape(b, t, DN_WIDTH).astype(x.dtype) @ w_out

def shared_kv(x, kv_w):
    b, t, _ = x.shape
    kv = x @ kv_w
    keys = kv[..., :DA_QK_WIDTH].reshape(b, t, DA_HEADS, 2, DA_HEAD_DIM).transpose(3, 0, 2, 1, 4)
    vals = kv[..., DA_QK_WIDTH:].reshape(b, t, DA_HEADS, DA_V_DIM).transpose(0, 2, 1, 3)
    return keys, vals

def differential_attention(x, keys, vals, w_q, lam_p, subln_w, w_out, lam_init):
    b, t, _ = x.shape
    nb = t // Q_BLOCK
    q = (x @ w_q).reshape(b, nb, Q_BLOCK, DA_HEADS, 2, DA_HEAD_DIM).transpose(1, 4, 0, 3, 2, 5)
    lp = lam_p.astype(jnp.float32)
    lam = jnp.exp(jnp.sum(lp[0] * lp[1])) - jnp.exp(jnp.sum(lp[2] * lp[3])) + lam_init
    key_pos = jnp.arange(t)
    scale = DA_HEAD_DIM ** -0.5

    def block(args):
        q_blk, blk = args
        query_pos = blk * Q_BLOCK + jnp.arange(Q_BLOCK)
        mask = key_pos[None, :] <= query_pos[:, None]
        s = jnp.einsum('sbhqd,sbhkd->sbhqk', q_blk, keys).astype(jnp.float32) * scale
        p = jax.nn.softmax(jnp.where(mask, s, -jnp.inf), axis=-1)
        a = p[0] - lam * p[1]
        return jnp.einsum('bhqk,bhkv->bhqv', a.astype(vals.dtype), vals)

    o = lax.map(block, (q, jnp.arange(nb)))
    o = o.transpose(1, 0, 3, 2, 4).reshape(b, t, DA_HEADS, DA_V_DIM)
    o = rms_norm(o, subln_w) * (1.0 - lam_init)
    return o.reshape(b, t, DA_WIDTH).astype(x.dtype) @ w_out

def hierarchical_moe(x, w_group, w_expert, w13, w2):
    b, t, d = x.shape
    n = b * t
    m = n * TOP_K
    xf = x.reshape(n, d)
    group_prob = jax.nn.softmax((xf @ w_group).astype(jnp.float32), axis=-1)
    p_group, group_idx = lax.top_k(group_prob, 1)
    expert_logits = (xf @ w_expert).astype(jnp.float32).reshape(n, N_GROUPS, EXPERTS_PER_GROUP)
    in_group = expert_logits[jnp.arange(n), group_idx[:, 0]]
    top_p, top_i = lax.top_k(jax.nn.softmax(in_group, axis=-1), TOP_K)
    gate = (p_group * top_p / jnp.sum(top_p, axis=-1, keepdims=True)).reshape(m)
    expert_id = (group_idx * EXPERTS_PER_GROUP + top_i).reshape(m)
    token_id = jnp.repeat(jnp.arange(n), TOP_K)
    order = jnp.argsort(expert_id)
    eid_s, tok_s, gate_s = expert_id[order], token_id[order], gate[order]
    counts = jnp.bincount(expert_id, length=N_EXPERTS)
    start = jnp.cumsum(counts) - counts
    padded = (counts + MOE_BLOCK - 1) // MOE_BLOCK * MOE_BLOCK
    pad_end = jnp.cumsum(padded)
    pad_start = pad_end - padded
    dest = pad_start[eid_s] + jnp.arange(m) - start[eid_s]
    n_rows = (m + N_EXPERTS * (MOE_BLOCK - 1) + MOE_BLOCK - 1) // MOE_BLOCK * MOE_BLOCK
    n_blocks = n_rows // MOE_BLOCK
    row_tok = jnp.zeros((n_rows,), jnp.int32).at[dest].set(tok_s)
    row_gate = jnp.zeros((n_rows,), x.dtype).at[dest].set(gate_s.astype(x.dtype))
    block_eid = jnp.minimum(jnp.searchsorted(pad_end, jnp.arange(n_blocks) * MOE_BLOCK, side='right'),
                            N_EXPERTS - 1)
    x_rows = xf[row_tok].reshape(n_blocks, MOE_BLOCK, d)

    def expert_block(args):
        xb, e = args
        hcat = xb @ w13[e]
        hid = jax.nn.silu(hcat[:, :EXPERT_FF]) * hcat[:, EXPERT_FF:]
        return hid @ w2[e]

    y_rows = lax.map(expert_block, (x_rows, block_eid)).reshape(n_rows, d)
    y = jax.ops.segment_sum(y_rows * row_gate[:, None], row_tok, num_segments=n)
    return y.reshape(b, t, d)

def lambda_init(layer_idx):
    return 0.8 - 0.6 * math.exp(-0.3 * layer_idx)

def first_inputs(seed: int = 0) -> dict:
    key = jax.random.key(seed)
    ks = jax.random.split(key, 24)
    f32 = jnp.float32
    D = D_MODEL

    def nrm(k, shape, scale):
        return jax.random.normal(k, shape, f32) * scale

    in_a = 4 * DN_WIDTH + 2 * DN_HEADS
    x = nrm(ks[0], (BATCH, SEQ, D), 1.0)
    a_w_in = nrm(ks[1], (N_A_LAYERS, D, in_a), D ** -0.5)
    a_conv_w = nrm(ks[2], (N_A_LAYERS, CONV_K, 3 * DN_WIDTH), CONV_K ** -0.5)
    a_a_log = jnp.log(jax.random.uniform(ks[3], (N_A_LAYERS, DN_HEADS), f32, 1.0, 16.0))
    dt = jnp.exp(jax.random.uniform(ks[4], (N_A_LAYERS, DN_HEADS), f32, math.log(1e-3), math.log(1e-1)))
    a_dt_bias = dt + jnp.log(-jnp.expm1(-dt))
    a_norm_w = 1.0 + nrm(ks[5], (N_A_LAYERS, DN_HEAD_DIM), 0.02)
    a_w_out = nrm(ks[6], (N_A_LAYERS, DN_WIDTH, D), DN_WIDTH ** -0.5 * BETA_INIT)
    kv_w = nrm(ks[7], (D, DA_QK_WIDTH + DA_WIDTH), D ** -0.5)
    b_w_q = nrm(ks[8], (N_B_LAYERS, D, DA_QK_WIDTH), D ** -0.5)
    b_lambda = nrm(ks[9], (N_B_LAYERS, 4, DA_HEAD_DIM), 0.1)
    b_subln_w = 1.0 + nrm(ks[10], (N_B_LAYERS, DA_V_DIM), 0.02)
    b_w_out = nrm(ks[11], (N_B_LAYERS, DA_WIDTH, D), DA_WIDTH ** -0.5 * BETA_INIT)
    ln_mix_g = 1.0 + nrm(ks[12], (DEPTH, D), 0.02)
    ln_mix_b = nrm(ks[13], (DEPTH, D), 0.02)
    ln_ffn_g = 1.0 + nrm(ks[14], (DEPTH, D), 0.02)
    ln_ffn_b = nrm(ks[15], (DEPTH, D), 0.02)
    moe_w_group = nrm(ks[16], (DEPTH, D, N_GROUPS), D ** -0.5)
    moe_w_expert = nrm(ks[17], (DEPTH, D, N_EXPERTS), D ** -0.5)
    moe_w13 = nrm(ks[18], (DEPTH, N_EXPERTS, D, 2 * EXPERT_FF), D ** -0.5)
    moe_w2 = nrm(ks[19], (DEPTH, N_EXPERTS, EXPERT_FF, D), EXPERT_FF ** -0.5 * BETA_INIT)
    return {'x': x, 'a_w_in': a_w_in, 'a_conv_w': a_conv_w, 'a_a_log': a_a_log, 'a_dt_bias': a_dt_bias,
            'a_norm_w': a_norm_w, 'a_w_out': a_w_out, 'kv_w': kv_w, 'b_w_q': b_w_q, 'b_lambda': b_lambda,
            'b_subln_w': b_subln_w, 'b_w_out': b_w_out, 'ln_mix_g': ln_mix_g, 'ln_mix_b': ln_mix_b,
            'ln_ffn_g': ln_ffn_g, 'ln_ffn_b': ln_ffn_b, 'moe_w_group': moe_w_group,
            'moe_w_expert': moe_w_expert, 'moe_w13': moe_w13, 'moe_w2': moe_w2}

def first_block(x, a_w_in, a_conv_w, a_a_log, a_dt_bias, a_norm_w, a_w_out, kv_w, b_w_q, b_lambda,
              b_subln_w, b_w_out, ln_mix_g, ln_mix_b, ln_ffn_g, ln_ffn_b, moe_w_group, moe_w_expert,
              moe_w13, moe_w2):
    h = x
    keys, vals = None, None
    for layer in range(DEPTH):
        if layer < N_A_LAYERS:
            mix = gated_deltanet(h, a_w_in[layer], a_conv_w[layer], a_a_log[layer], a_dt_bias[layer],
                                 a_norm_w[layer], a_w_out[layer])
        else:
            j = layer - N_A_LAYERS
            if j == 0:
                keys, vals = shared_kv(h, kv_w)
            mix = differential_attention(h, keys, vals, b_w_q[j], b_lambda[j], b_subln_w[j], b_w_out[j],
                                         lambda_init(layer))
        h = layer_norm(ALPHA * h + mix, ln_mix_g[layer], ln_mix_b[layer])
        ffn = hierarchical_moe(h, moe_w_group[layer], moe_w_expert[layer], moe_w13[layer], moe_w2[layer])
        h = layer_norm(ALPHA * h + ffn, ln_ffn_g[layer], ln_ffn_b[layer])
    return h


DEPTH_2 = 4

N_MIXERS = 3
ALPHA_2 = (2.0 * DEPTH_2) ** 0.25
BETA = (8.0 * DEPTH_2) ** -0.25
HEAD_NORM_EPS = 1e-6

HGRN_EXPAND = 128
HGRN_HEADS = D_MODEL // HGRN_EXPAND
HGRN_DK = HGRN_EXPAND
HGRN_DV = D_MODEL // HGRN_HEADS
HGRN_CHUNK = 64

MLSTM_HEADS = 8
MLSTM_DV = D_MODEL // MLSTM_HEADS
MLSTM_DQK = MLSTM_DV // 2
MLSTM_CONV = 4
MLSTM_CHUNK = 64
MLSTM_QK_W = MLSTM_HEADS * MLSTM_DQK
MLSTM_IN_W = 2 * MLSTM_QK_W + 2 * D_MODEL + 2 * MLSTM_HEADS

S5_GROUP_CH = 16
S5_GROUPS = D_MODEL // S5_GROUP_CH
S5_STATE = 64
S5_CHUNK = 1024
S5_DT_MIN = 1e-3
S5_DT_MAX = 1e-1

FFN_HIDDEN = -(-8 * D_MODEL // (3 * 256)) * 256

N_HGRN = (DEPTH_2 + 2) // 3
N_MLSTM = (DEPTH_2 + 1) // 3
N_S5 = DEPTH_2 // 3


def _layernorm(x, g, b):
    xf = x.astype(jnp.float32)
    mu = jnp.mean(xf, axis=-1, keepdims=True)
    xc = xf - mu
    var = jnp.mean(xc * xc, axis=-1, keepdims=True)
    return (xc * lax.rsqrt(var + LN_EPS) * g + b).astype(x.dtype)

def _head_rmsnorm(h, w):
    return h * lax.rsqrt(jnp.mean(h * h, axis=-1, keepdims=True) + HEAD_NORM_EPS) * w

def _to_chunks(t, n_heads, chunk):
    bsz, seq, width = t.shape
    return t.reshape(bsz, seq // chunk, chunk, n_heads, width // n_heads).transpose(1, 0, 3, 2, 4)

def _from_chunks(t):
    nc, bsz, h, c, d = t.shape
    return t.transpose(1, 0, 3, 2, 4).reshape(bsz, nc * c, h, d)

def _causal_conv(u, w):
    k_w = w.shape[0]
    seq = u.shape[1]
    up = jnp.pad(u, ((0, 0), (k_w - 1, 0), (0, 0)))
    out = up[:, 0:seq] * w[0]
    for j in range(1, k_w):
        out = out + up[:, j:j + seq] * w[j]
    return out

def _hgrn_lower_bounds(lb_logits):
    p = jax.nn.softmax(lb_logits.astype(jnp.float32), axis=0)
    c = jnp.cumsum(p, axis=0)
    return c - c[0:1]

def _hgrn2_mixer(x, w_in, norm_w, w_out, lb):
    bsz, seq, _ = x.shape
    q, f, v, g = jnp.split(x @ w_in, 4, axis=-1)
    f = f.astype(jnp.float32)
    log_f = jnp.logaddexp(jnp.log(lb), jnp.log1p(-lb) + jax.nn.log_sigmoid(f))
    k = (1.0 - lb) * jax.nn.sigmoid(-f)
    q = jax.nn.silu(q.astype(jnp.float32))
    qc = _to_chunks(q, HGRN_HEADS, HGRN_CHUNK)
    kc = _to_chunks(k, HGRN_HEADS, HGRN_CHUNK)
    vc = _to_chunks(v.astype(jnp.float32), HGRN_HEADS, HGRN_CHUNK)
    lfc = _to_chunks(log_f, HGRN_HEADS, HGRN_CHUNK)
    mask = jnp.tril(jnp.ones((HGRN_CHUNK, HGRN_CHUNK), dtype=bool))

    def step(s_prev, inp):
        qb, kb, vb, lfb = inp
        b = jnp.cumsum(lfb, axis=2)
        diff = b[:, :, :, None, :] - b[:, :, None, :, :]
        decay = jnp.exp(jnp.where(mask[:, :, None], diff, -jnp.inf))
        att = jnp.einsum('bhtd,bhsd,bhtsd->bhts', qb, kb, decay)
        o = jnp.einsum('bhts,bhse->bhte', att, vb) + jnp.einsum('bhtd,bhde->bhte', qb * jnp.exp(b), s_prev)
        b_last = b[:, :, -1]
        k_dec = kb * jnp.exp(b_last[:, :, None, :] - b)
        s_new = jnp.exp(b_last)[..., None] * s_prev + jnp.einsum('bhsd,bhse->bhde', k_dec, vb)
        return s_new, o

    s0 = jnp.zeros((bsz, HGRN_HEADS, HGRN_DK, HGRN_DV), jnp.float32)
    _, oc = lax.scan(step, s0, (qc, kc, vc, lfc))
    o = _head_rmsnorm(_from_chunks(oc), norm_w.astype(jnp.float32))
    o = o.reshape(bsz, seq, D_MODEL) * jax.nn.silu(g.astype(jnp.float32))
    return o.astype(x.dtype) @ w_out

def _mlstm_mixer(x, w_in, conv_w, gate_b, norm_w, w_out):
    bsz, seq, _ = x.shape
    proj = x @ w_in
    qk = proj[..., :2 * MLSTM_QK_W]
    v = proj[..., 2 * MLSTM_QK_W:2 * MLSTM_QK_W + D_MODEL]
    o_pre = proj[..., 2 * MLSTM_QK_W + D_MODEL:2 * MLSTM_QK_W + 2 * D_MODEL]
    gates = proj[..., 2 * MLSTM_QK_W + 2 * D_MODEL:].astype(jnp.float32) + gate_b.astype(jnp.float32)
    qk = jax.nn.silu(_causal_conv(qk, conv_w).astype(jnp.float32))
    q = qk[..., :MLSTM_QK_W]
    k = qk[..., MLSTM_QK_W:] * (MLSTM_DQK ** -0.5)
    log_i = gates[..., :MLSTM_HEADS]
    log_f = jax.nn.log_sigmoid(gates[..., MLSTM_HEADS:])
    qc = _to_chunks(q, MLSTM_HEADS, MLSTM_CHUNK)
    kc = _to_chunks(k, MLSTM_HEADS, MLSTM_CHUNK)
    vc = _to_chunks(v.astype(jnp.float32), MLSTM_HEADS, MLSTM_CHUNK)
    lic = _to_chunks(log_i, MLSTM_HEADS, MLSTM_CHUNK)[..., 0]
    lfc = _to_chunks(log_f, MLSTM_HEADS, MLSTM_CHUNK)[..., 0]
    mask = jnp.tril(jnp.ones((MLSTM_CHUNK, MLSTM_CHUNK), dtype=bool))

    def step(carry, inp):
        c_prev, n_prev, m_prev = carry
        qb, kb, vb, lib, lfb = inp
        b = jnp.cumsum(lfb, axis=-1)
        log_d = jnp.where(mask, b[..., :, None] - b[..., None, :] + lib[..., None, :], -jnp.inf)
        log_inter = b + m_prev[..., None]
        m_t = jnp.maximum(jnp.max(log_d, axis=-1), log_inter)
        d_mat = jnp.exp(log_d - m_t[..., None])
        w_inter = jnp.exp(log_inter - m_t)
        s = jnp.einsum('bhtd,bhsd->bhts', qb, kb) * d_mat
        num = jnp.einsum('bhts,bhse->bhte', s, vb) + w_inter[..., None] * jnp.einsum('bhtd,bhde->bhte', qb, c_prev)
        den = jnp.sum(s, axis=-1) + w_inter * jnp.einsum('bhtd,bhd->bht', qb, n_prev)
        h = num / jnp.maximum(jnp.abs(den), jnp.exp(-m_t))[..., None]
        b_last = b[..., -1]
        log_w = b_last[..., None] - b + lib
        m_new = jnp.maximum(b_last + m_prev, jnp.max(log_w, axis=-1))
        w_s = jnp.exp(log_w - m_new[..., None])
        w_prev = jnp.exp(b_last + m_prev - m_new)
        c_new = w_prev[..., None, None] * c_prev + jnp.einsum('bhs,bhsd,bhse->bhde', w_s, kb, vb)
        n_new = w_prev[..., None] * n_prev + jnp.einsum('bhs,bhsd->bhd', w_s, kb)
        return (c_new, n_new, m_new), h

    init = (jnp.zeros((bsz, MLSTM_HEADS, MLSTM_DQK, MLSTM_DV), jnp.float32),
            jnp.zeros((bsz, MLSTM_HEADS, MLSTM_DQK), jnp.float32),
            jnp.zeros((bsz, MLSTM_HEADS), jnp.float32))
    _, hc = lax.scan(step, init, (qc, kc, vc, lic, lfc))
    h = _head_rmsnorm(_from_chunks(hc), norm_w.astype(jnp.float32).reshape(MLSTM_HEADS, MLSTM_DV))
    h = h.reshape(bsz, seq, D_MODEL) * jax.nn.sigmoid(o_pre.astype(jnp.float32))
    return h.astype(x.dtype) @ w_out

def _cmul(ar, ai, br, bi):
    return ar * br - ai * bi, ar * bi + ai * br

def _s5_combine(e1, e2):
    a1r, a1i, b1r, b1i = e1
    a2r, a2i, b2r, b2i = e2
    ar, ai = _cmul(a2r, a2i, a1r, a1i)
    tr, ti = _cmul(a2r, a2i, b1r, b1i)
    return ar, ai, tr + b2r, ti + b2i

def _s5_mixer(x, w_in, a_re, a_im, log_dt, b_re, b_im, c_re, c_im, d_skip, w_out):
    bsz, seq, _ = x.shape
    f32 = jnp.float32
    u = (x @ w_in).astype(f32)
    a_re = a_re.astype(f32)
    a_im = a_im.astype(f32)
    b_re = b_re.astype(f32)
    b_im = b_im.astype(f32)
    c_re = c_re.astype(f32)
    c_im = c_im.astype(f32)
    dt = jnp.exp(log_dt.astype(f32))[:, None]
    mag = jnp.exp(a_re * dt)
    abar_re = mag * jnp.cos(a_im * dt)
    abar_im = mag * jnp.sin(a_im * dt)
    nr = abar_re - 1.0
    ni = abar_im
    den = a_re * a_re + a_im * a_im
    coef_re = (nr * a_re + ni * a_im) / den
    coef_im = (ni * a_re - nr * a_im) / den
    bbar_re = coef_re[..., None] * b_re - coef_im[..., None] * b_im
    bbar_im = coef_re[..., None] * b_im + coef_im[..., None] * b_re
    chunk = math.gcd(seq, S5_CHUNK)
    nc = seq // chunk
    ug = u.reshape(bsz, nc, chunk, S5_GROUPS, S5_GROUP_CH).transpose(1, 0, 2, 3, 4)
    a_r = jnp.broadcast_to(abar_re, (bsz, chunk, S5_GROUPS, S5_STATE))
    a_i = jnp.broadcast_to(abar_im, (bsz, chunk, S5_GROUPS, S5_STATE))

    def step(carry, ub):
        hr, hi = carry
        bu_re = jnp.einsum('blgc,gpc->blgp', ub, bbar_re)
        bu_im = jnp.einsum('blgc,gpc->blgp', ub, bbar_im)
        pr, pi, sr, si = lax.associative_scan(_s5_combine, (a_r, a_i, bu_re, bu_im), axis=1)
        cr, ci = _cmul(pr, pi, hr[:, None], hi[:, None])
        sr = sr + cr
        si = si + ci
        y = jnp.einsum('blgp,gcp->blgc', sr, c_re) - jnp.einsum('blgp,gcp->blgc', si, c_im)
        return (sr[:, -1], si[:, -1]), y

    h0 = (jnp.zeros((bsz, S5_GROUPS, S5_STATE), f32), jnp.zeros((bsz, S5_GROUPS, S5_STATE), f32))
    _, yc = lax.scan(step, h0, ug)
    y = yc.transpose(1, 0, 2, 3, 4).reshape(bsz, seq, D_MODEL)
    y = y + d_skip.astype(f32) * u
    y = jax.nn.gelu(y).astype(x.dtype)
    za, zb = jnp.split(y @ w_out, 2, axis=-1)
    return za * jax.nn.sigmoid(zb)

def _swiglu(x, w_gate_up, w_down):
    gate, up = jnp.split(x @ w_gate_up, 2, axis=-1)
    return (jax.nn.silu(gate) * up) @ w_down

def second_inputs(seed: int = 0) -> dict:
    key = jax.random.key(seed)
    ks = jax.random.split(key, 24)
    D = D_MODEL
    nrm = jax.random.normal
    x = nrm(ks[0], (BATCH, SEQ, D), jnp.float32)
    hgrn_w_in = nrm(ks[1], (N_HGRN, D, 4 * D), jnp.float32) * D ** -0.5
    hgrn_norm_w = 1.0 + 0.02 * nrm(ks[2], (N_HGRN, HGRN_DV), jnp.float32)
    hgrn_w_out = nrm(ks[3], (N_HGRN, D, D), jnp.float32) * (D ** -0.5 * BETA)
    hgrn_lb_logits = 0.5 * nrm(ks[4], (DEPTH_2, HGRN_HEADS * HGRN_DK), jnp.float32)
    mlstm_w_in = nrm(ks[5], (N_MLSTM, D, MLSTM_IN_W), jnp.float32) * D ** -0.5
    mlstm_conv_w = nrm(ks[6], (N_MLSTM, MLSTM_CONV, 2 * MLSTM_QK_W), jnp.float32) * MLSTM_CONV ** -0.5
    i_bias = 0.1 * nrm(ks[7], (N_MLSTM, MLSTM_HEADS), jnp.float32)
    f_bias = jnp.linspace(3.0, 6.0, MLSTM_HEADS, dtype=jnp.float32)[None] + 0.1 * nrm(ks[8], (N_MLSTM, MLSTM_HEADS), jnp.float32)
    mlstm_gate_b = jnp.concatenate([i_bias, f_bias], axis=-1)
    mlstm_norm_w = 1.0 + 0.02 * nrm(ks[9], (N_MLSTM, D), jnp.float32)
    mlstm_w_out = nrm(ks[10], (N_MLSTM, D, D), jnp.float32) * (D ** -0.5 * BETA)
    s5_w_in = nrm(ks[11], (N_S5, D, D), jnp.float32) * D ** -0.5
    s5_a_re = -0.5 + 0.01 * nrm(ks[12], (N_S5, S5_GROUPS, S5_STATE), jnp.float32)
    s5_a_im = (jnp.pi * jnp.arange(S5_STATE, dtype=jnp.float32))[None, None] + 0.01 * nrm(ks[13], (N_S5, S5_GROUPS, S5_STATE), jnp.float32)
    s5_log_dt = jax.random.uniform(ks[14], (N_S5, S5_GROUPS), jnp.float32, math.log(S5_DT_MIN), math.log(S5_DT_MAX))
    s5_b_re = nrm(ks[15], (N_S5, S5_GROUPS, S5_STATE, S5_GROUP_CH), jnp.float32) * (2 * S5_GROUP_CH) ** -0.5
    s5_b_im = nrm(ks[16], (N_S5, S5_GROUPS, S5_STATE, S5_GROUP_CH), jnp.float32) * (2 * S5_GROUP_CH) ** -0.5
    s5_c_re = nrm(ks[17], (N_S5, S5_GROUPS, S5_GROUP_CH, S5_STATE), jnp.float32) * S5_STATE ** -0.5
    s5_c_im = nrm(ks[18], (N_S5, S5_GROUPS, S5_GROUP_CH, S5_STATE), jnp.float32) * S5_STATE ** -0.5
    s5_d = nrm(ks[19], (N_S5, D), jnp.float32)
    s5_w_out = nrm(ks[20], (N_S5, D, 2 * D), jnp.float32) * (D ** -0.5 * BETA)
    ffn_w_gate_up = nrm(ks[21], (DEPTH_2, D, 2 * FFN_HIDDEN), jnp.float32) * D ** -0.5
    ffn_w_down = nrm(ks[22], (DEPTH_2, FFN_HIDDEN, D), jnp.float32) * (FFN_HIDDEN ** -0.5 * BETA)
    kg, kb = jax.random.split(ks[23])
    ln_g = 1.0 + 0.02 * nrm(kg, (DEPTH_2, 2, D), jnp.float32)
    ln_b = 0.02 * nrm(kb, (DEPTH_2, 2, D), jnp.float32)
    return {"x": x, "hgrn_w_in": hgrn_w_in, "hgrn_norm_w": hgrn_norm_w, "hgrn_w_out": hgrn_w_out,
            "hgrn_lb_logits": hgrn_lb_logits, "mlstm_w_in": mlstm_w_in, "mlstm_conv_w": mlstm_conv_w,
            "mlstm_gate_b": mlstm_gate_b, "mlstm_norm_w": mlstm_norm_w, "mlstm_w_out": mlstm_w_out,
            "s5_w_in": s5_w_in, "s5_a_re": s5_a_re, "s5_a_im": s5_a_im, "s5_log_dt": s5_log_dt,
            "s5_b_re": s5_b_re, "s5_b_im": s5_b_im, "s5_c_re": s5_c_re, "s5_c_im": s5_c_im,
            "s5_d": s5_d, "s5_w_out": s5_w_out, "ffn_w_gate_up": ffn_w_gate_up, "ffn_w_down": ffn_w_down,
            "ln_g": ln_g, "ln_b": ln_b}

def second_block(x, hgrn_w_in, hgrn_norm_w, hgrn_w_out, hgrn_lb_logits, mlstm_w_in, mlstm_conv_w,
              mlstm_gate_b, mlstm_norm_w, mlstm_w_out, s5_w_in, s5_a_re, s5_a_im, s5_log_dt,
              s5_b_re, s5_b_im, s5_c_re, s5_c_im, s5_d, s5_w_out, ffn_w_gate_up, ffn_w_down,
              ln_g, ln_b):
    lb_all = _hgrn_lower_bounds(hgrn_lb_logits)
    for i in range(DEPTH_2):
        kind = i % N_MIXERS
        j = i // N_MIXERS
        if kind == 0:
            h = _hgrn2_mixer(x, hgrn_w_in[j], hgrn_norm_w[j], hgrn_w_out[j], lb_all[i])
        elif kind == 1:
            h = _mlstm_mixer(x, mlstm_w_in[j], mlstm_conv_w[j], mlstm_gate_b[j], mlstm_norm_w[j], mlstm_w_out[j])
        else:
            h = _s5_mixer(x, s5_w_in[j], s5_a_re[j], s5_a_im[j], s5_log_dt[j], s5_b_re[j], s5_b_im[j],
                          s5_c_re[j], s5_c_im[j], s5_d[j], s5_w_out[j])
        x = _layernorm(ALPHA_2 * x + h, ln_g[i, 0], ln_b[i, 0])
        x = _layernorm(ALPHA_2 * x + _swiglu(x, ffn_w_gate_up[i], ffn_w_down[i]), ln_g[i, 1], ln_b[i, 1])
    return x


def setup_inputs(seed=0):
    out = dict(first_inputs(seed))
    for name, value in second_inputs(seed + 1).items():
        if name != "x":
            out[name + "_2"] = value
    return out


def reference(
    x, a_w_in, a_conv_w, a_a_log, a_dt_bias, a_norm_w, a_w_out, kv_w, b_w_q, b_lambda,
    b_subln_w, b_w_out, ln_mix_g, ln_mix_b, ln_ffn_g, ln_ffn_b, moe_w_group, moe_w_expert,
    moe_w13, moe_w2, hgrn_w_in_2, hgrn_norm_w_2, hgrn_w_out_2, hgrn_lb_logits_2, mlstm_w_in_2,
    mlstm_conv_w_2, mlstm_gate_b_2, mlstm_norm_w_2, mlstm_w_out_2, s5_w_in_2, s5_a_re_2,
    s5_a_im_2, s5_log_dt_2, s5_b_re_2, s5_b_im_2, s5_c_re_2, s5_c_im_2, s5_d_2, s5_w_out_2,
    ffn_w_gate_up_2, ffn_w_down_2, ln_g_2, ln_b_2,
):
    x = first_block(
        x, a_w_in, a_conv_w, a_a_log, a_dt_bias, a_norm_w, a_w_out, kv_w, b_w_q, b_lambda,
        b_subln_w, b_w_out, ln_mix_g, ln_mix_b, ln_ffn_g, ln_ffn_b, moe_w_group, moe_w_expert,
        moe_w13, moe_w2,
    )
    return second_block(
        x, hgrn_w_in_2, hgrn_norm_w_2, hgrn_w_out_2, hgrn_lb_logits_2, mlstm_w_in_2,
        mlstm_conv_w_2, mlstm_gate_b_2, mlstm_norm_w_2, mlstm_w_out_2, s5_w_in_2, s5_a_re_2,
        s5_a_im_2, s5_log_dt_2, s5_b_re_2, s5_b_im_2, s5_c_re_2, s5_c_im_2, s5_d_2, s5_w_out_2,
        ffn_w_gate_up_2, ffn_w_down_2, ln_g_2, ln_b_2,
    )


_drawn_inputs = setup_inputs


def setup_inputs(seed=0):
    import zlib

    import numpy as np

    out = dict(_drawn_inputs(seed))
    spreads = {}
    factors = {'a_norm_w': 6.704,
     'b_lambda': 6.588,
     'b_subln_w': 5.939,
     'hgrn_norm_w_2': 8.0,
     'hgrn_lb_logits_2': 5.995,
     'mlstm_norm_w_2': 22.124,
     's5_a_re_2': 64.0,
     's5_a_im_2': 64.0,
     's5_log_dt_2': 64.0,
     's5_b_re_2': 64.0,
     's5_b_im_2': 64.0,
     's5_c_re_2': 64.0,
     's5_c_im_2': 64.0}
    for name, (base, spread) in spreads.items():
        noise = np.random.default_rng([zlib.crc32(name.encode()), seed]).standard_normal(out[name].shape)
        drawn = base * np.exp(spread * noise) if base else spread * noise
        out[name] = __import__('jax').numpy.asarray(drawn.astype(out[name].dtype))
    for name, factor in factors.items():
        out[name] = (out[name] * factor).astype(out[name].dtype)
    return out
```

```python
import math
from contextlib import ExitStack

import numpy as np

import concourse.bass as bass
from concourse import mybir

F32 = mybir.dt.float32
BF16 = mybir.dt.bfloat16
I16 = mybir.dt.int16
I32 = mybir.dt.int32
ALU = mybir.AluOpType
ACT = mybir.ActivationFunctionType
AX = mybir.AxisListType

P = 128
T = 256
TT = T // P
D = 1024
KT = D // P
H = 8
HD = D // H
CONV = 4
N_GROUPS, PER_GROUP = 4, 8
N_EXP = N_GROUPS * PER_GROUP
FF_E = D // 2
FF = -(-8 * D // (3 * 256)) * 256
S5_G, S5_N, S5_C = D // 16, 64, 16
S5_TILES = S5_G * S5_N // P
LN_EPS, RMS_EPS = 1e-5, 1e-6
ALPHA_FIRST, ALPHA_SECOND = (2 * 2) ** 0.25, (2.0 * 4) ** 0.25
LAM_INIT = 0.8 - 0.6 * math.exp(-0.3 * 1)
BIG = 1e30

RING = 12
COLS = 256
UNIT = KT * COLS
FT = COLS // P
SLOTS = 4


class Jobs:

    def __init__(self):
        self.of, self.readers, self.banks, self.bank_before = {}, [], [], []
        self.nth, self.last = [], {}
        self.n_read = {"act": 0, "dve": 0}

    def declare(self, stage, table, banks):
        for turn, (name, i, reader) in enumerate(table):
            j = len(self.readers)
            bank = banks[turn % len(banks)]
            self.of[stage, name, i] = j
            self.readers.append(reader)
            self.banks.append(bank)
            self.bank_before.append(self.last.get(bank))
            self.last[bank] = j
            self.n_read[reader] += 1
            self.nth.append(self.n_read[reader])


class Count:

    def __init__(self):
        self.n = 0

    def next(self):
        self.n += 1
        return self.n


def tiles_of(table, n, reader):
    return [(table, i, reader) for i in range(n)]


def build(nc, W, out):
    ctx = ExitStack()
    with ctx:
        jobs = Jobs()
        sems, counts = {}, {}

        def sem(name):
            if name not in sems:
                sems[name] = ctx.enter_context(nc.semaphore(name))
            return sems[name]

        def sb(name, shape, dt=F32):
            return ctx.enter_context(nc.sbuf_tensor(name, shape, dt))

        def done(name):
            counts[name] = counts.get(name, 0) + 1
            return counts[name]

        act_step, dve_step, pool_step = sem("act_step"), sem("dve_step"), sem("pool_step")
        act_steps, dve_steps, pool_steps = Count(), Count(), Count()
        act_took, dve_took, psum_ready = sem("act_took"), sem("dve_took"), sem("psum_ready")
        act_reads, dve_reads = Count(), Count()

        psum = ctx.enter_context(nc.psum_tensor("psum", [P, 8, 512], F32))
        acc = psum[:, 4:8, :].rearrange("p (t b) n -> p t (b n)", t=TT)
        FOUR, EIGHT = list(range(4)), list(range(8))

        def job(stage, name, i=0):
            return jobs.of[stage, name, i] + 1

        def bank_of(stage, name, i=0):
            return psum[:, jobs.banks[jobs.of[stage, name, i]], :]

        def taken(stage, name, i=0):
            j = jobs.of[stage, name, i]
            return act_took if jobs.readers[j] == "act" else dve_took, jobs.nth[j]

        def bank_free(stage, name, i=0):
            before = jobs.bank_before[jobs.of[stage, name, i]]
            if before is None:
                return sem("masks_ready"), 1
            return act_took if jobs.readers[before] == "act" else dve_took, jobs.nth[before]

        ring = sb("ring", [P, RING, UNIT])
        h = sb("h", [P, TT, D])
        hT = sb("hT", [P, KT, T])
        SCR = 10
        scratch = sb("scratch", [P, SCR, UNIT])
        ln_gb = scratch[:, SCR - 1, :].rearrange("p (k d) -> p k d", k=2)
        ident = sb("ident", [P, P])
        ones = sb("ones", [P, P])
        causal = sb("causal", [P, P])
        strict = sb("strict", [P, P], BF16)
        LEVELS = [1, 2, 4, 8, 16, 32, 64]
        level = sb("level", [P, len(LEVELS), P], BF16)
        dn_gate_w = sb("dn_gate_w", [P, KT, 2 * H])
        ml_gate_w = sb("ml_gate_w", [P, KT, 2 * H])
        router_w = sb("router_w", [P, 2, KT, N_GROUPS + N_EXP])
        rows = scratch[:, SCR - 1, 0:2 * P].rearrange("p (a n) -> p a n", a=2)
        vecs = sb("vecs", [P, 2, P])
        dn_norm_w = sb("dn_norm_w", [P, HD])
        da_norm_w = sb("da_norm_w", [P, HD])
        hg_norm_w = sb("hg_norm_w", [P, 2, HD])
        a_log = sb("a_log", [P, H])
        dt_bias = sb("dt_bias", [P, H])
        ml_gate_b = sb("ml_gate_b", [H, 2])
        lam_p = sb("lam_p", [P, 4, 64])
        small = sb("small", [P, 768])
        N_MIX_ROWS = CONV * 24
        conv_a = vecs[:, 0, 0:N_MIX_ROWS].rearrange("p (k c) -> p k c", k=CONV)
        conv_m = vecs[:, 0, N_MIX_ROWS:N_MIX_ROWS + CONV * 8].rearrange("p (k c) -> p k c", k=CONV)
        lb_log = vecs[:, 1, 0:32].rearrange("p (l c) -> p l c", l=4)
        s5_are, s5_aim, s5_d = vecs[:, 1, 32:64], vecs[:, 1, 64:96], vecs[:, 1, 96:104]

        def scr(b, n=UNIT, at=0):
            flat = scratch[:, :, :].rearrange("p b n -> p (b n)")
            return flat[:, b * UNIT + at:b * UNIT + at + n]

        def magnitude(v, dst, x):
            return v.scalar_tensor_tensor(out=dst, in0=x, scalar=-1.0, in1=x, op0=ALU.mult, op1=ALU.max)

        def heads(ap):
            return ap.rearrange("p (h n) -> p h n", h=H)

        def bc(ap, shape):
            return ap.unsqueeze(2).broadcast_to(shape)

        landed = [sem(f"landed{s}") for s in range(RING)]
        units, used = [], []

        def add_unit(load, done):
            units.append(load)
            used.append(done)
            return len(units) - 1

        def slot(n):
            return ring[:, n % RING, :]

        def k_unit(n):
            return slot(n).rearrange("p (j c) -> p j c", j=KT)

        def row_unit(n):
            return slot(n).rearrange("p (a n) -> p a n", a=FT)

        def await_unit(pe, n):
            pe.wait_ge(landed[n % RING], 16 * (n // RING + 1))

        def cols_of(w, c0):
            return lambda: w[:, c0:c0 + COLS].rearrange("(j p) n -> p j n", p=P)

        out_units = [0]
        OUT_UNIT = "out_unit_done"

        def add_projection(stage, name, w, c0, n):
            base = len(units)
            for i in range(n):
                j = jobs.of[stage, name, i]
                add_unit(cols_of(w, c0 + COLS * i), (psum_ready, j + 1))
            return base

        def add_out(w, n, c0=0):
            base = len(units)
            for i in range(n):
                out_units[0] += 1
                add_unit(cols_of(w, c0 + COLS * i), (sem(OUT_UNIT), out_units[0]))
            return base, out_units[0]

        def project_channels(pe, stage, name, n, base, src):
            for i in range(n):
                pe.wait_ge(*bank_free(stage, name, i))
                bank = bank_of(stage, name, i).rearrange("p (c t) -> p c t", c=2)
                await_unit(pe, base + i)
                w = k_unit(base + i)
                for c in range(2):
                    for j in range(KT):
                        mm = pe.matmul(bank[:, c, :], w[:, j, c * P:(c + 1) * P], src[:, j, :],
                                         start=(j == 0), stop=(j == KT - 1))
                mm.then_inc(psum_ready, 1)

        def project_tokens(pe, stage, name, n, base, src):
            for i in range(n):
                pe.wait_ge(*bank_free(stage, name, i))
                bank = bank_of(stage, name, i).rearrange("p (t c) -> p t c", t=TT)
                await_unit(pe, base + i)
                w = k_unit(base + i)
                for t in range(TT):
                    for j in range(KT):
                        mm = pe.matmul(bank[:, t, :], src[:, j, t * P:(t + 1) * P], w[:, j, :],
                                         start=(j == 0), stop=(j == KT - 1))
                mm.then_inc(psum_ready, 1)

        def project_out(pe, base, n, src):
            for i in range(n):
                await_unit(pe, base + i)
                w = k_unit(base + i)
                for t in range(TT):
                    for j in range(KT):
                        mm = pe.matmul(acc[:, t, i * COLS:(i + 1) * COLS], src[:, j, t * P:(t + 1) * P], w[:, j, :],
                                         start=(j == 0), stop=(j == KT - 1))
                mm.then_inc(sem(OUT_UNIT), 1)

        N_LN = 12

        def declare_turn(n):
            jobs.declare(f"turn{n}", tiles_of("hT", 4, "act"), FOUR)

        def turn_pe(pe, n):
            for t in range(TT):
                if n == 0:
                    if t == 0:
                        pe.wait_ge(sem("x_landed"), 16)
                        pe.wait_ge(sem("masks_ready"), 1)
                else:
                    pe.wait_ge(sem("ln_done"), 2 * (n - 1) + t + 1)
                for q in range(2):
                    pe.wait_ge(*bank_free(f"turn{n}", "hT", 2 * t + q))
                    bank = bank_of(f"turn{n}", "hT", 2 * t + q)
                    for c in range(4):
                        j = 4 * q + c
                        mm = pe.transpose(bank[:, c * P:(c + 1) * P], h[:, t, j * P:(j + 1) * P], ident[:, :])
                    mm.then_inc(psum_ready, 1)

        def turn_act(act, n):
            for t in range(TT):
                for q in range(2):
                    act.wait_ge(psum_ready, job(f"turn{n}", "hT", 2 * t + q))
                    bank = bank_of(f"turn{n}", "hT", 2 * t + q)
                    act.copy(hT[:, 4 * q:4 * q + 4, t * P:(t + 1) * P],
                                         bank.rearrange("p (c t) -> p c t", c=4)).then_inc(act_took, 1)
                    act.wait_ge(act_took, act_reads.next())

        def wait_turned(pe, n):
            pe.wait_ge(*taken(f"turn{n}", "hT", 3))

        bn_s = small[:, 0:24].rearrange("p (t c s) -> p t c s", t=TT, c=2)
        mean_var = small[:, 24:28].rearrange("p (t s) -> p t s", t=TT)
        ln_sd = small[:, 28:30]
        ln_rstd = small[:, 30:32]

        def ln_params(pool, n, g, b):
            before, count = {0: ("dn_normed", 1), 2: ("da_normed", 1), HG_LN[0]: ("hg_normed", 1), ML_TURN: ("ml_normed", 1),
                             S5_TURN: ("s5_gelu", KT), HG_LN[1]: ("hg_normed", 2)}.get(n, ("ln_done", 2 * n))
            pool.wait_ge(sem(before), count)
            pool.dma_start(ln_gb[:, 0, :], g.partition_broadcast(P)).then_inc(sem("ln_params_landed"), 16)
            pool.dma_start(ln_gb[:, 1, :], b.partition_broadcast(P)).then_inc(sem("ln_params_landed"), 16)

        def ln_dve(dve, n, alpha, wait_mix, mix=None):
            v = dve
            wait_mix(dve)
            for t in range(TT):
                src = acc[:, t, :] if mix is None else mix[:, t, :]
                v.scalar_tensor_tensor(out=h[:, t, :], in0=h[:, t, :], scalar=alpha, in1=src,
                                              op0=ALU.mult, op1=ALU.add).then_inc(dve_step, 1)
                dve.wait_ge(dve_step, dve_steps.next())
                for c in range(2):
                    v.bn_stats(bn_s[:, t, c, :], h[:, t, c * 512:(c + 1) * 512]).then_inc(dve_step, 1)
                    dve.wait_ge(dve_step, dve_steps.next())
                v.bn_aggr(mean_var[:, t, :], bn_s[:, t, :, :]).then_inc(dve_step, 1)
                dve.wait_ge(dve_step, dve_steps.next())
                v.tensor_scalar(mean_var[:, t, 1:2], mean_var[:, t, 1:2], LN_EPS, None, ALU.add).then_inc(sem("ln_var"), 1)
                dve.wait_ge(sem("ln_var"), done("ln_var"))
            dve.wait_ge(sem("ln_params_landed"), 32 * (n + 1))
            for t in range(TT):
                dve.wait_ge(sem("ln_sd_done"), 2 * n + t + 1)
                v.reciprocal(ln_rstd[:, t:t + 1], ln_sd[:, t:t + 1]).then_inc(dve_step, 1)
                dve.wait_ge(dve_step, dve_steps.next())
                v.tensor_scalar(h[:, t, :], h[:, t, :], mean_var[:, t, 0:1], ln_rstd[:, t:t + 1],
                                       ALU.subtract, ALU.mult).then_inc(dve_step, 1)
                dve.wait_ge(dve_step, dve_steps.next())
                v.tensor_tensor(h[:, t, :], h[:, t, :], ln_gb[:, 0, :], ALU.mult).then_inc(dve_step, 1)
                dve.wait_ge(dve_step, dve_steps.next())
                v.tensor_tensor(h[:, t, :], h[:, t, :], ln_gb[:, 1, :], ALU.add).then_inc(sem("ln_done"), 1)
                dve.wait_ge(sem("ln_done"), done("ln_done"))

        def ln_act(act, n):
            for t in range(TT):
                act.wait_ge(sem("ln_var"), 2 * n + t + 1)
                act.activation(ln_sd[:, t:t + 1], mean_var[:, t, 1:2], ACT.Sqrt).then_inc(sem("ln_sd_done"), 1)
                act.wait_ge(sem("ln_sd_done"), done("ln_sd_done"))

        glu_steps = [0]
        silu_b = [scr(8, 512), scr(8, 512, 512)]
        hid_b = [scr(8, 512, 1024), scr(8, 512, 1536)]
        gate_bc = scr(0, N_EXP * T)

        class Glu:

            def __init__(self, n, src, gated):
                self.n, self.src, self.gated = n, src, gated
                self.g0 = glu_steps[0]
                self.m0 = sum(g.n for g in glus if g.gated)
                glus.append(self)
                glu_steps[0] += n
                self.loops = (n - 3) // SLOTS
                self.base = len(units)
                order = [("gate", 0), ("up", 0), ("gate", 1), ("up", 1), ("down", 0)]
                for s in range(2, n):
                    order += [("gate", s), ("up", s), ("down", s - 1)]
                order += [("down", n - 1)]
                self.order = order
                self.at = {}
                for kind, s in order:
                    self.at[kind, s] = add_unit((self, kind, s), self.done(kind, s))

            def done(self, kind, s):
                name = {"gate": "glu_gate_ready", "up": "glu_up_ready", "down": "glu_down_done"}[kind]
                return sem(name), s + (self.g0 + 1)

            def unit(self, kind, s, i=0):
                n = self.at[kind, s]
                return n, i * 16 + 16 * (n // RING + 1)

        glus = []

        def glu_pe_up(pe, g, s, i=0):
            step = i * SLOTS + s
            if not isinstance(s, int) or s >= 2:
                pe.wait_ge(sem("glu_hid_done"), step + (g.g0 - 1))
            for kind, b, name in (("gate", 2 * (s % 2), "glu_gate_ready"), ("up", 2 * (s % 2) + 1, "glu_up_ready")):
                n, value = g.unit(kind, s, i)
                pe.wait_ge(landed[n % RING], value)
                w = k_unit(n)
                bank = psum[:, b, :].rearrange("p (f t) -> p f t", f=FT)
                for f in range(FT):
                    for j in range(KT):
                        mm = pe.matmul(bank[:, f, :], w[:, j, f * P:(f + 1) * P], hT[:, j, :],
                                         start=(j == 0), stop=(j == KT - 1))
                mm.then_inc(sem(name), 1)

        def glu_pe_down(pe, g, s, i=0):
            step = i * SLOTS + s
            pe.wait_ge(sem("glu_hid_done"), step + (g.g0 + 1))
            n, value = g.unit("down", s, i)
            pe.wait_ge(landed[n % RING], value)
            w = row_unit(n)
            hid = hid_b[s % 2].rearrange("p (f t) -> p f t", f=FT)
            for t in range(TT):
                for c in range(2):
                    for f in range(FT):
                        mm = pe.matmul(acc[:, t, c * 512:(c + 1) * 512], hid[:, f, t * P:(t + 1) * P],
                                         w[:, f, c * 512:(c + 1) * 512],
                                         start=(s == 0 and f == 0), stop=(s == g.n - 1 and f == FT - 1))
            mm.then_inc(sem("glu_down_done"), 1)

        def glu_pe(pe, g):
            glu_pe_up(pe, g, 0)
            glu_pe_up(pe, g, 1)
            glu_pe_down(pe, g, 0)
            with pe.Fori(0, g.loops) as i:
                for k in range(SLOTS):
                    glu_pe_up(pe, g, 2 + k, i)
                    glu_pe_down(pe, g, 1 + k, i)
            for s in range(2 + SLOTS * g.loops, g.n):
                glu_pe_up(pe, g, s)
                glu_pe_down(pe, g, s - 1)
            glu_pe_down(pe, g, g.n - 1)

        def glu_silu(act, g, s, i=0):
            step = i * SLOTS + s
            act.wait_ge(sem("glu_gate_ready"), step + (g.g0 + 1))
            if s >= 2:
                act.wait_ge(sem("glu_hid_done"), step + (g.g0 - 1))
            act.activation(silu_b[s % 2], psum[:, 2 * (s % 2), :], ACT.Silu).then_inc(sem("glu_silu_done"), 1)

        def glu_hid(dve, g, s, i=0):
            v = dve
            step = i * SLOTS + s
            sg, hid = silu_b[s % 2], hid_b[s % 2]
            dve.wait_ge(sem("glu_silu_done"), step + (g.g0 + 1))
            if s >= 2:
                dve.wait_ge(sem("glu_down_done"), step + (g.g0 - 1))
            if g.gated:
                gate = gate_bc[:, bass.ds(i * (2 * T) + (s // 2) * T, T)]
                v.tensor_tensor(hid.rearrange("p (f t) -> p f t", f=FT), sg.rearrange("p (f t) -> p f t", f=FT),
                                gate.unsqueeze(1).broadcast_to([P, FT, T]), ALU.mult)\
                    .then_inc(sem("glu_gated"), 1)
                dve.wait_ge(sem("glu_gated"), step + (g.m0 + 1))
                sg = hid
            dve.wait_ge(sem("glu_up_ready"), step + (g.g0 + 1))
            v.tensor_tensor(hid, sg, psum[:, 2 * (s % 2) + 1, :], ALU.mult).then_inc(sem("glu_hid_done"), 1)

        def glu_steps_of(eng, g, one):
            for s in range(2):
                one(eng, g, s)
            with eng.Fori(0, g.loops) as i:
                for k in range(SLOTS):
                    one(eng, g, 2 + k, i)
            for s in range(2 + SLOTS * g.loops, g.n):
                one(eng, g, s)

        def wait_glu(g):
            return lambda eng: eng.wait_ge(sem("glu_down_done"), g.g0 + g.n)

        def ffn_src(layer):
            w1, w2 = W["ffn_w_gate_up_2"], W["ffn_w_down_2"]

            def src(kind, s, i):
                if kind == "down":
                    return w2[layer, bass.ds(i * (SLOTS * COLS) + s * COLS, COLS), :]\
                        .rearrange("(a p) n -> p a n", p=P)
                c0 = s * COLS + (FF if kind == "up" else 0)
                return w1[layer, :, bass.ds(i * (SLOTS * COLS) + c0, COLS)].rearrange("(j p) n -> p j n", p=P)
            return src

        def moe_src(layer):
            w1, w2 = W["moe_w13"], W["moe_w2"]
            per = FF_E // COLS

            def src(kind, s, i):
                e = bass.ds(i * (SLOTS // per) + s // per, 1)
                at = (s % per) * COLS
                if kind == "down":
                    return w2[layer, e, at:at + COLS, :].rearrange("e (a p) n -> p (e a) n", p=P)
                at += FF_E if kind == "up" else 0
                return w1[layer, e, :, at:at + COLS].rearrange("e (j p) n -> p (e j) n", p=P)
            return src

        def load_unit(sp, n, src, value=None):
            dst = k_unit(n) if src.shape[1] == KT else row_unit(n)
            sp.dma_start(dst, src).then_inc(landed[n % RING], 16)

        def load_straight(sp, n):
            if n >= RING:
                sp.wait_ge(*used[n - RING])
            load = units[n]
            load_unit(sp, n, load() if callable(load) else load[0].src(load[1], load[2], 0))

        def sp_loads(sp):
            n = 0
            while n < len(units):
                g = units[n]
                if callable(g):
                    load_straight(sp, n)
                    n += 1
                    continue
                g = g[0]
                first = g.at["gate", 2]
                for m in range(n, first + 3 * SLOTS):
                    load_straight(sp, m)
                with sp.Fori(1, g.loops) as i:
                    for m in range(first, first + 3 * SLOTS):
                        _, kind, s = units[m]
                        name, value = g.done(kind, s)
                        sp.wait_ge(name, i * SLOTS + (value - SLOTS))
                        load_unit(sp, m, g.src(kind, s, i))
                n = first + 3 * SLOTS * g.loops
                while n < len(units) and not callable(units[n]) and units[n][0] is g:
                    load_straight(sp, n)
                    n += 1

        jobs.declare("setup", tiles_of("vecs", 2, "dve"), EIGHT)
        ROWS = [P, 104]
        N_PARAMS = 0

        def setup_pool(pool):
            nonlocal N_PARAMS
            g = pool

            def param(dst, src):
                nonlocal N_PARAMS
                N_PARAMS += 1
                g.dma_start(dst, src, allow_slow_non_contiguous=True).then_inc(sem("params_landed"), 16)

            g.memset(ident[:, :], 0.0).then_inc(pool_step, 1)
            pool.wait_ge(pool_step, pool_steps.next())
            g.affine_select(out=ident[:, :], in_=ident[:, :], compare_op=ALU.not_equal, fill=1.0, base=0,
                                    pattern=[[-1, P]], channel_multiplier=1).then_inc(pool_step, 1)
            pool.wait_ge(pool_step, pool_steps.next())
            g.memset(ones[:, :], 1.0).then_inc(pool_step, 1)
            pool.wait_ge(pool_step, pool_steps.next())
            for m, op in ((causal, ALU.is_ge), (strict, ALU.is_gt)):
                g.affine_select(out=m[:, :], in_=ones[:, :], compare_op=op, fill=0.0, base=0,
                                        pattern=[[1, P]], channel_multiplier=-1).then_inc(pool_step, 1)
                pool.wait_ge(pool_step, pool_steps.next())
            g.memset(level[:, :, :], 0.0).then_inc(pool_step, 1)
            pool.wait_ge(pool_step, pool_steps.next())
            for n, m in enumerate(LEVELS):
                nb = P // (2 * m)
                v = level[:, n, :].rearrange("p (b f r) -> p b f r", f=2, r=m)[:, :, 1, :]
                g.memset(v, 1.0).then_inc(pool_step, 1)
                pool.wait_ge(pool_step, pool_steps.next())
                g.affine_select(out=v, in_=v, compare_op=ALU.is_ge, fill=0.0, base=0,
                                        pattern=[[-2 * m, nb], [0, m]], channel_multiplier=1).then_inc(pool_step, 1)
                pool.wait_ge(pool_step, pool_steps.next())
                last = g.affine_select(out=v, in_=v, compare_op=ALU.is_ge, fill=0.0, base=m - 1,
                                       pattern=[[2 * m, nb], [0, m]], channel_multiplier=-1)
                if n < len(LEVELS) - 1:
                    last.then_inc(pool_step, 1)
                    pool.wait_ge(pool_step, pool_steps.next())
            last.then_inc(sem("masks_ready"), 1)
            pool.wait_ge(sem("masks_ready"), done("masks_ready"))
            param(rows[0:N_MIX_ROWS, 0, :], W["a_conv_w"][0].rearrange("k (c p) -> (k c) p", p=P))
            param(rows[N_MIX_ROWS:P, 0, :], W["mlstm_conv_w_2"][0].rearrange("k (c p) -> (k c) p", p=P))
            param(rows[0:32, 1, :], W["hgrn_lb_logits_2"].rearrange("l (c p) -> (l c) p", p=P))
            param(rows[32:64, 1, :], W["s5_a_re_2"][0].rearrange("(j g) p -> j (g p)", g=2))
            param(rows[64:96, 1, :], W["s5_a_im_2"][0].rearrange("(j g) p -> j (g p)", g=2))
            param(rows[96:104, 1, :], W["s5_d_2"][0].rearrange("(c p) -> c p", p=P))
            param(dn_gate_w[:, :, :], W["a_w_in"][0, :, 4 * D:4 * D + 2 * H].rearrange("(j p) n -> p j n", p=P))
            param(a_log[:, :], W["a_a_log"][0].partition_broadcast(P))
            param(dt_bias[:, :], W["a_dt_bias"][0].partition_broadcast(P))
            param(dn_norm_w[:, :], W["a_norm_w"][0].partition_broadcast(P))
            for n in range(2):
                param(router_w[:, n, :, 0:N_GROUPS], W["moe_w_group"][n].rearrange("(j p) n -> p j n", p=P))
                param(router_w[:, n, :, N_GROUPS:], W["moe_w_expert"][n].rearrange("(j p) n -> p j n", p=P))
            param(da_norm_w[:, :], W["b_subln_w"][0].partition_broadcast(P))
            param(lam_p[:, :, :].rearrange("p a n -> p (a n)"),
                  W["b_lambda"][0].rearrange("a n -> (a n)").partition_broadcast(P))
            for n in range(2):
                param(hg_norm_w[:, n, :], W["hgrn_norm_w_2"][n].partition_broadcast(P))
            param(ml_gate_w[:, :, :], W["mlstm_w_in_2"][0, :, 3 * D:3 * D + 2 * H].rearrange("(j p) n -> p j n", p=P))
            param(ml_gate_b[:, :], W["mlstm_gate_b_2"][0].rearrange("(a h) -> h a", a=2))

        def wait_params(eng):
            eng.wait_ge(sem("params_landed"), 16 * 20)

        def setup_pe(pe):
            wait_params(pe)
            pe.wait_ge(sem("masks_ready"), 1)
            for i, n in enumerate(ROWS):
                pe.wait_ge(*bank_free("setup", "vecs", i))
                bank = bank_of("setup", "vecs", i)
                pe.transpose(bank[:, 0:n], rows[0:n, i, :], ident[0:n, 0:n]).then_inc(psum_ready, 1)

        def setup_dve(dve):
            wait_params(dve)
            for i, n in enumerate(ROWS):
                dve.wait_ge(psum_ready, job("setup", "vecs", i))
                bank = bank_of("setup", "vecs", i)
                dve.tensor_copy(vecs[:, i, 0:n], bank[:, 0:n]).then_inc(dve_took, 1)
                dve.wait_ge(dve_took, dve_reads.next())

        def conv_silu(dve, act_in, dst, taps):
            v = dve
            v.tensor_scalar(dst, act_in[:, 0:T], taps[0], None, ALU.mult).then_inc(dve_step, 1)
            dve.wait_ge(dve_step, dve_steps.next())
            for k in range(1, CONV):
                last = v.scalar_tensor_tensor(out=dst, in0=act_in[:, k:k + T], scalar=taps[k], in1=dst,
                                              op0=ALU.mult, op1=ALU.add)
                if k < CONV - 1:
                    last.then_inc(dve_step, 1)
                    dve.wait_ge(dve_step, dve_steps.next())
            return last

        def declare_head_norm(stage):
            return tiles_of("oT", 4, "act")

        def head_norm_dve(dve, stage, o, tmp, st, w, gate, eps, scale=1.0):
            v = dve
            o16, tmp16 = (x.rearrange("p (a n) -> p a n", n=HD) for x in (o, tmp))
            v.tensor_tensor(tmp, o, o, ALU.mult).then_inc(dve_step, 1)
            dve.wait_ge(dve_step, dve_steps.next())
            v.tensor_reduce(st[:, 0, :], tmp16, AX.X, ALU.add).then_inc(dve_step, 1)
            dve.wait_ge(dve_step, dve_steps.next())
            v.tensor_scalar(st[:, 0, :], st[:, 0, :], 1.0 / HD, eps, ALU.mult, ALU.add).then_inc(sem(f"{stage}_ms"), 1)
            dve.wait_ge(sem(f"{stage}_ms"), done(f"{stage}_ms"))
            dve.wait_ge(sem(f"{stage}_rms"), counts[f"{stage}_ms"])
            v.reciprocal(st[:, 2, :], st[:, 1, :]).then_inc(dve_step, 1)
            dve.wait_ge(dve_step, dve_steps.next())
            if scale != 1.0:
                v.tensor_scalar(st[:, 2, :], st[:, 2, :], scale, None, ALU.mult).then_inc(dve_step, 1)
                dve.wait_ge(dve_step, dve_steps.next())
            v.tensor_tensor(o16, o16, bc(st[:, 2, :], [P, 2 * H, HD]), ALU.mult).then_inc(dve_step, 1)
            dve.wait_ge(dve_step, dve_steps.next())
            if w is not None:
                last = v.tensor_tensor(o16, o16, w, ALU.mult)
                if gate is not None:
                    last.then_inc(dve_step, 1)
                    dve.wait_ge(dve_step, dve_steps.next())
            if gate is not None:
                last = v.tensor_tensor(o, o, gate, ALU.mult)
            last.then_inc(sem(f"{stage}_normed"), 1)
            dve.wait_ge(sem(f"{stage}_normed"), done(f"{stage}_normed"))

        def head_norm_act(act, stage, st, nth=1):
            act.wait_ge(sem(f"{stage}_ms"), nth)
            act.activation(st[:, 1, :], st[:, 0, :], ACT.Sqrt).then_inc(sem(f"{stage}_rms"), 1)
            act.wait_ge(sem(f"{stage}_rms"), done(f"{stage}_rms"))

        def o_turn_pe(pe, key, stage, o, nth=1):
            pe.wait_ge(sem(f"{stage}_normed"), nth)
            o3 = o.rearrange("p (t d) -> p t d", t=TT)
            for i in range(4):
                pe.wait_ge(*bank_free(key, "oT", i))
                bank = bank_of(key, "oT", i)
                for c in range(4):
                    j = 4 * (i % 2) + c
                    mm = pe.transpose(bank[:, c * P:(c + 1) * P], o3[:, i // 2, j * P:(j + 1) * P], ident[:, :])
                mm.then_inc(psum_ready, 1)

        def o_turn_act(act, key, oT):
            for i in range(4):
                act.wait_ge(psum_ready, job(key, "oT", i))
                bank = bank_of(key, "oT", i)
                q = 4 * (i % 2)
                act.copy(oT[:, q:q + 4, (i // 2) * P:(i // 2 + 1) * P],
                                     bank.rearrange("p (c t) -> p c t", c=4)).then_inc(act_took, 1)
                act.wait_ge(act_took, act_reads.next())

        def declare_dn():
            t = tiles_of("qkv", 12, "act") + tiles_of("z", 4, "act") + tiles_of("gate", 1, "dve")
            t += tiles_of("ss", 8, "act") + tiles_of("gc", 1, "dve") + tiles_of("v", 4, "dve")
            t += tiles_of("rowgc", 4, "dve") + tiles_of("rowbeta", 4, "dve")
            for i in range(4):
                t += [("kk", i, "dve"), ("qk", i, "dve")]
            t += tiles_of("x0", 4, "act")
            for n in range(1, len(LEVELS)):
                t += [("t1", 4 * n + g, "act") for g in range(4)]
                for g in range(4):
                    if n < len(LEVELS) - 1:
                        t += [("u", 4 * n + g, "dve")]
                    t += [("ut", 4 * n + g, "dve")]
            for name, reader in (("kdec", "act"), ("u0", "act"), ("S", "act"), ("kS", "dve"), ("u1", "act"),
                                 ("qS", "act"), ("o0", "dve"), ("o1", "dve")):
                t += tiles_of(name, 2, reader)
            jobs.declare("dn", t + declare_head_norm("dn"), EIGHT)

        qT, kT, vT, v_tok, zs = (scr(n) for n in range(5))
        pad = [scr(8, 2 * 260), scr(8, 2 * 260, 520)]
        dn_nrm = [scr(9, 512), scr(9, 512, 512)]
        DT, DB, AT, attnT, X, XT = scr(8), scr(9), scr(5), scr(2), scr(6), scr(7)
        T1, ATl = scr(8), scr(9)
        kdec, S_dn, u0, u1, qSe, o_dn = scr(9, D), scr(9, D, D), scr(5, D), scr(5, D, D), scr(8, D), scr(6)
        dn_oT = scr(0).rearrange("p (j t) -> p j t", j=KT)

        def m16(x):
            return x.rearrange("p (m n) -> p m n", n=P)

        def th(x):
            return x.rearrange("p (t h) -> p t h", t=TT)
        st_h = small[:, 32:80].rearrange("p (a n) -> p a n", a=3)
        gl = small[:, 80:112].rearrange("p (t n) -> p t n", t=TT)
        dn_abs, dn_eb, dn_ea, dn_ln = (th(small[:, 112 + 16 * n:128 + 16 * n]) for n in range(4))
        beta, g_dn, gc, egc, beg = (th(small[:, 176 + 16 * n:192 + 16 * n]) for n in range(5))
        e_alog, g_sum, kd = small[:, 256:264], small[:, 264:272], small[:, 272:280]

        def dn_pe(pe, base):
            e = pe
            wait_turned(pe, 0)
            project_channels(pe, "dn", "qkv", 12, base, hT)
            project_tokens(pe, "dn", "z", 4, base + 12, hT)
            pe.wait_ge(*bank_free("dn", "gate"))
            bank = bank_of("dn", "gate")
            for t in range(TT):
                for j in range(KT):
                    mm = e.matmul(bank[:, t * 2 * H:(t + 1) * 2 * H], hT[:, j, t * P:(t + 1) * P], dn_gate_w[:, j, :],
                                  start=(j == 0), stop=(j == KT - 1))
            mm.then_inc(psum_ready, 1)
            for i in range(8):
                pe.wait_ge(sem("dn_sq"), i + 1)
                pe.wait_ge(*bank_free("dn", "ss", i))
                bank = bank_of("dn", "ss", i)
                e.matmul(bank, ones[:, :], dn_sq[i % 2], start=True, stop=True).then_inc(psum_ready, 1)
            pe.wait_ge(*bank_free("dn", "gc"))
            bank = bank_of("dn", "gc")
            pe.wait_ge(sem("dn_g"), 1)
            for t in range(TT):
                e.matmul(bank[:, t * H:(t + 1) * H], causal[:, :], g_dn[:, t, :], start=True, stop=True)
            e.matmul(bank[:, 2 * H:3 * H], ones[:, :], g_dn[:, 0, :], start=True, stop=True).then_inc(psum_ready, 1)
            pe.wait_ge(sem("dn_v"), 4)
            vT8 = heads(vT)
            for i in range(4):
                pe.wait_ge(*bank_free("dn", "v", i))
                bank = bank_of("dn", "v", i)
                for c in range(4):
                    hd = 4 * (i % 2) + c
                    mm = e.transpose(bank[:, c * P:(c + 1) * P], vT8[:, hd, (i // 2) * P:(i // 2 + 1) * P], ident[:, :])
                mm.then_inc(psum_ready, 1)
            for name, src, m in (("rowgc", g_dn, causal), ("rowbeta", beta, ident)):
                for i in range(4):
                    pe.wait_ge(*bank_free("dn", name, i))
                    bank = bank_of("dn", name, i)
                    for c in range(4):
                        hd = 4 * (i % 2) + c
                        mm = e.matmul(bank[:, c * P:(c + 1) * P], src[:, i // 2, hd:hd + 1].broadcast_to([P, P]),
                                      m[:, :], start=True, stop=True)
                    mm.then_inc(psum_ready, 1)
            pe.wait_ge(sem("dn_qk"), 8)
            q8, k8 = heads(qT), heads(kT)
            for i in range(4):
                ts = slice((i // 2) * P, (i // 2 + 1) * P)
                for name, r in (("kk", k8), ("qk", q8)):
                    pe.wait_ge(*bank_free("dn", name, i))
                    bank = bank_of("dn", name, i)
                    for c in range(4):
                        hd = 4 * (i % 2) + c
                        mm = e.matmul(bank[:, c * P:(c + 1) * P], k8[:, hd, ts], r[:, hd, ts], start=True, stop=True)
                    mm.then_inc(psum_ready, 1)
            A_, X_, XT_, T1_ = m16(ATl), m16(X), m16(XT), m16(T1)
            for i in range(4):
                pe.wait_ge(sem("dn_xt"), i + 1)
                pe.wait_ge(*bank_free("dn", "x0", i))
                bank = bank_of("dn", "x0", i)
                for c in range(4):
                    mm = e.transpose(bank[:, c * P:(c + 1) * P], XT_[:, 4 * i + c, :], ident[:, :])
                mm.then_inc(psum_ready, 1)
            for n in range(1, len(LEVELS)):
                for g in range(4):
                    pe.wait_ge(sem("dn_level"), 4 * (n - 1) + g + 1)
                    if n == 1:
                        pe.wait_ge(*taken("dn", "x0", g))
                    else:
                        pe.wait_ge(*taken("dn", "ut", 4 * (n - 1) + g))
                    pe.wait_ge(*bank_free("dn", "t1", 4 * n + g))
                    bank = bank_of("dn", "t1", 4 * n + g)
                    for c in range(4):
                        m = 4 * g + c
                        mm = e.matmul(bank[:, c * P:(c + 1) * P], A_[:, m, :], X_[:, m, :], start=True, stop=True)
                    mm.then_inc(psum_ready, 1)
                for g in range(4):
                    pe.wait_ge(*taken("dn", "t1", 4 * n + g))
                    if n < len(LEVELS) - 1:
                        pe.wait_ge(*bank_free("dn", "u", 4 * n + g))
                        bank = bank_of("dn", "u", 4 * n + g)
                        for c in range(4):
                            m = 4 * g + c
                            mm = e.matmul(bank[:, c * P:(c + 1) * P], XT_[:, m, :], T1_[:, m, :], start=True, stop=True)
                        mm.then_inc(psum_ready, 1)
                    pe.wait_ge(*bank_free("dn", "ut", 4 * n + g))
                    bank = bank_of("dn", "ut", 4 * n + g)
                    for c in range(4):
                        m = 4 * g + c
                        mm = e.matmul(bank[:, c * P:(c + 1) * P], T1_[:, m, :], XT_[:, m, :], start=True, stop=True)
                    mm.then_inc(psum_ready, 1)

            def four(name, i, one, wait=None):
                if wait:
                    wait(i)
                pe.wait_ge(*bank_free("dn", name, i))
                bank = bank_of("dn", name, i)
                for c in range(4):
                    hd = 4 * i + c
                    mm = one(bank[:, c * P:(c + 1) * P], hd)
                mm.then_inc(psum_ready, 1)

            v8 = v_tok.rearrange("p (t h n) -> p t h n", t=TT, h=H)
            kd8, S8, u0_8, u1_8, at16 = heads(kdec), heads(S_dn), heads(u0), heads(u1), m16(attnT)
            t0, t1 = slice(0, P), slice(P, T)

            def product(lhsT, rhs):
                return lambda o, hd: e.matmul(o, lhsT(hd), rhs(hd), start=True, stop=True)

            pe.wait_ge(*taken("dn", "ut", 4 * len(LEVELS) - 1))
            for i in range(2):
                four("kdec", i, lambda o, hd: e.transpose(o, k8[:, hd, t0], ident[:, :]))
            for i in range(2):
                four("u0", i, product(lambda hd: XT_[:, hd, :], lambda hd: v8[:, 0, hd, :]))
            for i in range(2):
                four("S", i, product(lambda hd: kd8[:, hd, :], lambda hd: u0_8[:, hd, :]),
                     lambda i: (pe.wait_ge(*taken("dn", "kdec", i)), pe.wait_ge(*taken("dn", "u0", i))))
            for i in range(2):
                four("kS", i, product(lambda hd: k8[:, hd, t1], lambda hd: S8[:, hd, :]),
                     lambda i: pe.wait_ge(*taken("dn", "S", i)))
            for i in range(2):
                four("u1", i, product(lambda hd: XT_[:, 8 + hd, :], lambda hd: v8[:, 1, hd, :]),
                     lambda i: pe.wait_ge(*taken("dn", "kS", i)))
            for i in range(2):
                four("qS", i, product(lambda hd: q8[:, hd, t1], lambda hd: S8[:, hd, :]))
            for i in range(2):
                four("o0", i, product(lambda hd: at16[:, hd, :], lambda hd: u0_8[:, hd, :]))
            for i in range(2):
                four("o1", i, product(lambda hd: at16[:, 8 + hd, :], lambda hd: u1_8[:, hd, :]),
                     lambda i: pe.wait_ge(*taken("dn", "u1", i)))
            o_turn_pe(pe, "dn", "dn", o_dn)

        dn_sq = [scr(5, 512), scr(5, 512, 512)]

        def dn_act(act):
            a = act
            for i in range(12):
                act.wait_ge(psum_ready, job("dn", "qkv", i))
                bank = bank_of("dn", "qkv", i)
                if i == 0:
                    act.wait_ge(sem("dn_pad_zero"), 1)
                if i >= 2:
                    act.wait_ge(sem("dn_conv"), 2 * (i - 1))
                p = pad[i % 2].rearrange("p (c n) -> p c n", c=2)
                a.copy(p[:, :, 3:3 + T], bank.rearrange("p (c n) -> p c n", c=2)).then_inc(act_took, 1)
                act.wait_ge(act_took, act_reads.next())
                if i >= 1:
                    dn_silu(act, i - 1)
            dn_silu(act, 11)
            for i in range(4):
                act.wait_ge(psum_ready, job("dn", "z", i))
                bank = bank_of("dn", "z", i)
                z = zs.rearrange("p (t d) -> p t d", t=TT)[:, :, i * COLS:(i + 1) * COLS]
                a.activation(z, bank.rearrange("p (t c) -> p t c", t=TT), ACT.Silu).then_inc(act_took, 1)
                act.wait_ge(act_took, act_reads.next())
            act.wait_ge(sem("dn_logits"), 1)
            a.activation(dn_eb, gl[:, :, 0:H], ACT.Exp, scale=-1.0).then_inc(act_step, 1)
            act.wait_ge(act_step, act_steps.next())
            a.activation(dn_ea, dn_abs, ACT.Exp, scale=-1.0).then_inc(act_step, 1)
            act.wait_ge(act_step, act_steps.next())
            a.activation(dn_ln, dn_ea, ACT.Ln, bias=1.0).then_inc(act_step, 1)
            act.wait_ge(act_step, act_steps.next())
            a.activation(e_alog, a_log[:, :], ACT.Exp).then_inc(sem("dn_gate_exp"), 1)
            act.wait_ge(sem("dn_gate_exp"), done("dn_gate_exp"))
            for i in range(8):
                act.wait_ge(psum_ready, job("dn", "ss", i))
                bank = bank_of("dn", "ss", i)
                if i >= 2:
                    act.wait_ge(sem("dn_qk"), i - 1)
                a.activation(dn_nrm[i % 2], bank, ACT.Sqrt, bias=rms_eps).then_inc(act_took, 1)
                act.wait_ge(act_took, act_reads.next())
            act.wait_ge(*taken("dn", "rowgc", 3))
            a.activation(DT, DT, ACT.Exp).then_inc(sem("dn_dt_exp"), 1)
            act.wait_ge(sem("dn_dt_exp"), done("dn_dt_exp"))
            act.wait_ge(*taken("dn", "gc"))
            a.activation(egc, gc, ACT.Exp).then_inc(act_step, 1)
            act.wait_ge(act_step, act_steps.next())
            act.wait_ge(sem("dn_kd"), 1)
            a.activation(kd, kd, ACT.Exp).then_inc(sem("dn_gc_exp"), 1)
            act.wait_ge(sem("dn_gc_exp"), done("dn_gc_exp"))
            for i in range(4):
                act.wait_ge(psum_ready, job("dn", "x0", i))
                bank = bank_of("dn", "x0", i)
                a.copy(X[:, 512 * i:512 * (i + 1)], bank).then_inc(act_took, 1)
                act.wait_ge(act_took, act_reads.next())
            for n in range(1, len(LEVELS)):
                for g in range(4):
                    act.wait_ge(psum_ready, job("dn", "t1", 4 * n + g))
                    bank = bank_of("dn", "t1", 4 * n + g)
                    if n == 1:
                        act.wait_ge(sem("dn_at"), 4)
                    a.copy(T1[:, 512 * g:512 * (g + 1)], bank).then_inc(act_took, 1)
                    act.wait_ge(act_took, act_reads.next())
            kd8 = heads(kdec)
            for i in range(2):
                act.wait_ge(psum_ready, job("dn", "kdec", i))
                bank = bank_of("dn", "kdec", i)
                for c in range(4):
                    last = a.activation(kd8[:, 4 * i + c, :], bank[:, c * P:(c + 1) * P], ACT.Copy,
                                        scale=kd[:, 4 * i + c:4 * i + c + 1])
                last.then_inc(act_took, 1)
                act.wait_ge(act_took, act_reads.next())
            for name, dst in (("u0", u0), ("S", S_dn), ("u1", u1)):
                for i in range(2):
                    act.wait_ge(psum_ready, job("dn", name, i))
                    bank = bank_of("dn", name, i)
                    a.copy(dst[:, 512 * i:512 * (i + 1)], bank).then_inc(act_took, 1)
                    act.wait_ge(act_took, act_reads.next())
            qs8 = heads(qSe)
            for i in range(2):
                act.wait_ge(psum_ready, job("dn", "qS", i))
                bank = bank_of("dn", "qS", i)
                for c in range(4):
                    last = a.activation(qs8[:, 4 * i + c, :], bank[:, c * P:(c + 1) * P], ACT.Copy,
                                        scale=egc[:, 1, 4 * i + c:4 * i + c + 1])
                last.then_inc(act_took, 1)
                act.wait_ge(act_took, act_reads.next())
            head_norm_act(act, "dn", st_h)
            o_turn_act(act, "dn", dn_oT)

        def dn_silu(act, i):
            act.wait_ge(sem("dn_conv"), 2 * (i + 1))
            dst = (qT, kT, vT)[i // 4][:, 512 * (i % 4):512 * (i % 4 + 1)]
            act.activation(dst, dst, ACT.Silu).then_inc(sem("dn_v" if i >= 8 else "dn_qk_silu"), 1)
            act.wait_ge(sem("dn_v" if i >= 8 else "dn_qk_silu"), done("dn_v" if i >= 8 else "dn_qk_silu"))

        rms_eps = small[:, 280:281]

        def dn_dve(dve):
            v = dve
            setup_dve(dve)
            v.memset(rms_eps, RMS_EPS).then_inc(dve_step, 1)
            dve.wait_ge(dve_step, dve_steps.next())
            for b in range(2):
                last = v.memset(pad[b].rearrange("p (c n) -> p c n", c=2)[:, :, 0:3], 0.0)
                if b == 0:
                    last.then_inc(dve_step, 1)
                    dve.wait_ge(dve_step, dve_steps.next())
            last.then_inc(sem("dn_pad_zero"), 1)
            dve.wait_ge(sem("dn_pad_zero"), done("dn_pad_zero"))
            for i in range(12):
                dve.wait_ge(*taken("dn", "qkv", i))
                p = pad[i % 2].rearrange("p (c n) -> p c n", c=2)
                for c in range(2):
                    ch = 2 * i + c
                    dst = (qT, kT, vT)[i // 4][:, T * (ch % 8):T * (ch % 8 + 1)]
                    conv_silu(dve, p[:, c, :], dst, [conv_a[:, k, ch:ch + 1] for k in range(CONV)]).then_inc(sem("dn_conv"), 1)
                    dve.wait_ge(sem("dn_conv"), done("dn_conv"))
            dve.wait_ge(psum_ready, job("dn", "gate"))
            bank = bank_of("dn", "gate")
            v.tensor_copy(gl, bank[:, 0:4 * H].rearrange("p (t n) -> p t n", t=TT)).then_inc(dve_took, 1)
            dve.wait_ge(dve_took, dve_reads.next())
            bh = lambda x: x.unsqueeze(1).broadcast_to([P, TT, H])
            al = gl[:, :, H:2 * H]
            v.tensor_tensor(al, al, bh(dt_bias[:, :]), ALU.add).then_inc(dve_step, 1)
            dve.wait_ge(dve_step, dve_steps.next())
            magnitude(v, dn_abs, al).then_inc(sem("dn_logits"), 1)
            dve.wait_ge(sem("dn_logits"), done("dn_logits"))
            for i in range(2):
                dn_square(dve, i)
            dve.wait_ge(sem("dn_gate_exp"), 1)
            v.tensor_scalar(dn_eb, dn_eb, 1.0, None, ALU.add).then_inc(dve_step, 1)
            dve.wait_ge(dve_step, dve_steps.next())
            v.reciprocal(beta, dn_eb).then_inc(dve_step, 1)
            dve.wait_ge(dve_step, dve_steps.next())
            v.tensor_scalar(al, al, 0.0, None, ALU.max).then_inc(dve_step, 1)
            dve.wait_ge(dve_step, dve_steps.next())
            v.tensor_tensor(al, al, dn_ln, ALU.add).then_inc(dve_step, 1)
            dve.wait_ge(dve_step, dve_steps.next())
            v.tensor_tensor(al, al, bh(e_alog), ALU.mult).then_inc(dve_step, 1)
            dve.wait_ge(dve_step, dve_steps.next())
            v.tensor_scalar(g_dn, al, -1.0, None, ALU.mult).then_inc(sem("dn_g"), 1)
            dve.wait_ge(sem("dn_g"), done("dn_g"))
            for i in range(8):
                dve.wait_ge(*taken("dn", "ss", i))
                x = (qT, kT)[i // 4][:, 512 * (i % 4):512 * (i % 4 + 1)]
                v.reciprocal(dn_nrm[i % 2], dn_nrm[i % 2]).then_inc(dve_step, 1)
                dve.wait_ge(dve_step, dve_steps.next())
                v.scalar_tensor_tensor(out=x, in0=dn_nrm[i % 2], scalar=HD ** -0.5 if i < 4 else 1.0, in1=x,
                                               op0=ALU.mult, op1=ALU.mult).then_inc(sem("dn_qk"), 1)
                dve.wait_ge(sem("dn_qk"), done("dn_qk"))
                if i + 2 < 8:
                    dn_square(dve, i + 2)
            dve.wait_ge(psum_ready, job("dn", "gc"))
            bank = bank_of("dn", "gc")
            v.tensor_copy(gc, th(bank[:, 0:2 * H])).then_inc(dve_step, 1)
            dve.wait_ge(dve_step, dve_steps.next())
            v.tensor_copy(g_sum, bank[:, 2 * H:3 * H]).then_inc(dve_took, 1)
            dve.wait_ge(dve_took, dve_reads.next())
            v.tensor_tensor(kd, g_sum, gc[:, 0, :], ALU.subtract).then_inc(sem("dn_kd"), 1)
            dve.wait_ge(sem("dn_kd"), done("dn_kd"))
            v8 = v_tok.rearrange("p (t h n) -> p t h n", t=TT, h=H)
            for i in range(4):
                dve.wait_ge(psum_ready, job("dn", "v", i))
                bank = bank_of("dn", "v", i)
                q = 4 * (i % 2)
                v.tensor_tensor(v8[:, i // 2, q:q + 4, :], bank.rearrange("p (c n) -> p c n", c=4),
                                          bc(beta[:, i // 2, q:q + 4], [P, 4, HD]), ALU.mult).then_inc(dve_took, 1)
                dve.wait_ge(dve_took, dve_reads.next())
            D16 = m16(DT)
            for i in range(4):
                dve.wait_ge(psum_ready, job("dn", "rowgc", i))
                bank = bank_of("dn", "rowgc", i)
                for c in range(4):
                    hd = 4 * (i % 2) + c
                    last = v.tensor_scalar(D16[:, 4 * i + c, :], bank[:, c * P:(c + 1) * P], gc[:, i // 2, hd:hd + 1],
                                           0.0, ALU.subtract, ALU.min)
                last.then_inc(dve_took, 1)
                dve.wait_ge(dve_took, dve_reads.next())
            dve.wait_ge(sem("dn_dt_exp"), 1)
            v.tensor_tensor(D16, D16, causal[:, :].unsqueeze(1).broadcast_to([P, 16, P]), ALU.mult).then_inc(dve_step, 1)
            dve.wait_ge(dve_step, dve_steps.next())
            B16 = m16(DB)
            v.tensor_tensor(B16, D16, strict[:, :].unsqueeze(1).broadcast_to([P, 16, P]), ALU.mult).then_inc(dve_step, 1)
            dve.wait_ge(dve_step, dve_steps.next())
            for i in range(4):
                dve.wait_ge(psum_ready, job("dn", "rowbeta", i))
                bank = bank_of("dn", "rowbeta", i)
                x = DB[:, 512 * i:512 * (i + 1)]
                v.tensor_tensor(x, x, bank, ALU.mult).then_inc(dve_took, 1)
                dve.wait_ge(dve_took, dve_reads.next())
            for i in range(4):
                x = slice(512 * i, 512 * (i + 1))
                dve.wait_ge(psum_ready, job("dn", "kk", i))
                bank = bank_of("dn", "kk", i)
                v.tensor_tensor(AT[:, x], bank, DB[:, x], ALU.mult).then_inc(dve_took, 1)
                dve.wait_ge(dve_took, dve_reads.next())
                dve.wait_ge(psum_ready, job("dn", "qk", i))
                bank = bank_of("dn", "qk", i)
                v.tensor_tensor(attnT[:, x], bank, DT[:, x], ALU.mult).then_inc(dve_took, 1)
                dve.wait_ge(dve_took, dve_reads.next())
                lv = level[:, 0, :].unsqueeze(1).broadcast_to([P, 4, P])
                idb = ident[:, :].unsqueeze(1).broadcast_to([P, 4, P])
                a4, x4 = m16(AT)[:, 4 * i:4 * i + 4, :], m16(XT)[:, 4 * i:4 * i + 4, :]
                v.tensor_tensor(x4, a4, lv, ALU.mult).then_inc(sem("dn_at"), 1)
                dve.wait_ge(sem("dn_at"), done("dn_at"))
                v.tensor_tensor(x4, idb, x4, ALU.subtract).then_inc(sem("dn_xt"), 1)
                dve.wait_ge(sem("dn_xt"), done("dn_xt"))
            for n in range(1, len(LEVELS)):
                for g in range(4):
                    lv = level[:, n, :].unsqueeze(1).broadcast_to([P, 4, P])
                    if n >= 2:
                        dve.wait_ge(psum_ready, job("dn", "t1", 4 * (n - 1) + g))
                    v.tensor_tensor(m16(ATl)[:, 4 * g:4 * g + 4, :], m16(AT)[:, 4 * g:4 * g + 4, :], lv, ALU.mult).then_inc(sem("dn_level"), 1)
                    dve.wait_ge(sem("dn_level"), done("dn_level"))
                for g in range(4):
                    x = slice(512 * g, 512 * (g + 1))
                    if n < len(LEVELS) - 1:
                        dve.wait_ge(psum_ready, job("dn", "u", 4 * n + g))
                        bank = bank_of("dn", "u", 4 * n + g)
                        v.tensor_tensor(X[:, x], X[:, x], bank, ALU.subtract).then_inc(dve_took, 1)
                        dve.wait_ge(dve_took, dve_reads.next())
                    dve.wait_ge(psum_ready, job("dn", "ut", 4 * n + g))
                    bank = bank_of("dn", "ut", 4 * n + g)
                    v.tensor_tensor(XT[:, x], XT[:, x], bank, ALU.subtract).then_inc(dve_took, 1)
                    dve.wait_ge(dve_took, dve_reads.next())
            dve.wait_ge(sem("dn_gc_exp"), 1)
            v.tensor_tensor(beg, beta, egc, ALU.mult).then_inc(dve_step, 1)
            dve.wait_ge(dve_step, dve_steps.next())
            v.tensor_scalar(beg, beg, -1.0, None, ALU.mult).then_inc(dve_step, 1)
            dve.wait_ge(dve_step, dve_steps.next())
            for i in range(2):
                dve.wait_ge(psum_ready, job("dn", "kS", i))
                bank = bank_of("dn", "kS", i)
                for c in range(4):
                    hd = 4 * i + c
                    last = v.scalar_tensor_tensor(out=v8[:, 1, hd, :], in0=bank[:, c * P:(c + 1) * P],
                                                  scalar=beg[:, 1, hd:hd + 1], in1=v8[:, 1, hd, :],
                                                  op0=ALU.mult, op1=ALU.add)
                last.then_inc(dve_took, 1)
                dve.wait_ge(dve_took, dve_reads.next())
            for i in range(2):
                dve.wait_ge(psum_ready, job("dn", "o0", i))
                bank = bank_of("dn", "o0", i)
                v.tensor_copy(o_dn[:, 512 * i:512 * (i + 1)], bank).then_inc(dve_took, 1)
                dve.wait_ge(dve_took, dve_reads.next())
            for i in range(2):
                dve.wait_ge(psum_ready, job("dn", "o1", i))
                bank = bank_of("dn", "o1", i)
                dve.wait_ge(*taken("dn", "qS", i))
                x = slice(512 * i, 512 * (i + 1))
                v.tensor_tensor(o_dn[:, D + 512 * i:D + 512 * (i + 1)], bank, qSe[:, x], ALU.add).then_inc(dve_took, 1)
                dve.wait_ge(dve_took, dve_reads.next())
            nw = dn_norm_w[:, :].unsqueeze(1).broadcast_to([P, 16, HD])
            head_norm_dve(dve, "dn", o_dn, scr(7), st_h, nw, zs, RMS_EPS)

        def dn_square(dve, i):
            if i == 0:
                dve.wait_ge(sem("dn_qk_silu"), 8)
            if i >= 2:
                dve.wait_ge(psum_ready, job("dn", "ss", i - 2))
            x = (qT, kT)[i // 4][:, 512 * (i % 4):512 * (i % 4 + 1)]
            dve.tensor_tensor(dn_sq[i % 2], x, x, ALU.mult).then_inc(sem("dn_sq"), 1)
            dve.wait_ge(sem("dn_sq"), done("dn_sq"))

        def declare_route(l):
            jobs.declare(f"route{l}", tiles_of("logits", 1, "dve") + tiles_of("gates", 16, "act"), FOUR)

        N_R = N_GROUPS + N_EXP
        r_lg = small[:, 288:360].rearrange("p (t n) -> p t n", t=TT)
        r_gmax, r_gsum, r_m1, r_m2, r_ex, r_f = (small[:, 360 + 2 * n:362 + 2 * n].unsqueeze(2) for n in range(6))
        r_ge, r_eq, r_om = (small[:, 376 + 8 * n:384 + 8 * n].rearrange("p (t n) -> p t n", t=TT) for n in range(3))
        r_cum = small[:, 400:464].rearrange("p (t n) -> p t n", t=TT)
        r_m, r_e1, r_e2 = (small[:, 464 + 64 * n:528 + 64 * n].rearrange("p (t n) -> p t n", t=TT) for n in range(3))
        r_gate = small[:, 656:720].rearrange("p (t n) -> p t n", t=TT)

        def route_pe(pe, l, turn):
            e = pe
            wait_turned(pe, turn)
            pe.wait_ge(*bank_free(f"route{l}", "logits"))
            bank = bank_of(f"route{l}", "logits")
            for t in range(TT):
                for j in range(KT):
                    mm = e.matmul(bank[:, t * N_R:(t + 1) * N_R], hT[:, j, t * P:(t + 1) * P], router_w[:, l, j, :],
                                  start=(j == 0), stop=(j == KT - 1))
            mm.then_inc(psum_ready, 1)
            pe.wait_ge(sem("route_gates"), l + 1)
            for i in range(16):
                pe.wait_ge(*bank_free(f"route{l}", "gates", i))
                bank = bank_of(f"route{l}", "gates", i)
                for c in range(2 * TT):
                    ex, t = 2 * i + c // TT, c % TT
                    mm = e.matmul(bank[:, c * P:(c + 1) * P], r_gate[:, t, ex:ex + 1].broadcast_to([P, P]), ident[:, :],
                                  start=True, stop=True)
                mm.then_inc(psum_ready, 1)
            for i in range(12, 16):
                pe.wait_ge(*taken(f"route{l}", "gates", i))

        def route_act(act, l):
            a = act
            act.wait_ge(sem("route_shift"), 2 * l + 1)
            a.activation(r_ge, r_ge, ACT.Exp).then_inc(sem("route_exp"), 1)
            act.wait_ge(sem("route_exp"), done("route_exp"))
            act.wait_ge(sem("route_shift"), 2 * l + 2)
            a.activation(r_ex, r_ex, ACT.Exp).then_inc(sem("route_exp"), 1)
            act.wait_ge(sem("route_exp"), done("route_exp"))
            for i in range(16):
                act.wait_ge(psum_ready, job(f"route{l}", "gates", i))
                bank = bank_of(f"route{l}", "gates", i)
                a.copy(gate_bc[:, 512 * i:512 * (i + 1)], bank).then_inc(act_took, 1)
                act.wait_ge(act_took, act_reads.next())

        def route_dve(dve, l):
            v = dve

            def first_of(eq, n):
                for t in range(TT):
                    v.tensor_tensor_scan(r_cum[:, t, 0:n], ones[:, 0:n], eq[:, t, :], 0.0, ALU.mult, ALU.add).then_inc(dve_step, 1)
                    dve.wait_ge(dve_step, dve_steps.next())
                v.tensor_scalar(r_cum[:, :, 0:n], r_cum[:, :, 0:n], 1.0, None, ALU.is_equal).then_inc(dve_step, 1)
                dve.wait_ge(dve_step, dve_steps.next())
                v.tensor_tensor(eq, eq, r_cum[:, :, 0:n], ALU.mult).then_inc(dve_step, 1)
                dve.wait_ge(dve_step, dve_steps.next())

            def over(x, n):
                return x.broadcast_to([P, TT, n])

            dve.wait_ge(psum_ready, job(f"route{l}", "logits"))
            bank = bank_of(f"route{l}", "logits")
            v.tensor_copy(r_lg, bank[:, 0:TT * N_R].rearrange("p (t n) -> p t n", t=TT)).then_inc(dve_took, 1)
            dve.wait_ge(dve_took, dve_reads.next())
            grp, exl = r_lg[:, :, 0:N_GROUPS], r_lg[:, :, N_GROUPS:]
            v.tensor_reduce(r_gmax, grp, AX.X, ALU.max).then_inc(dve_step, 1)
            dve.wait_ge(dve_step, dve_steps.next())
            v.tensor_tensor(r_ge, grp, over(r_gmax, N_GROUPS), ALU.subtract).then_inc(sem("route_shift"), 1)
            dve.wait_ge(sem("route_shift"), done("route_shift"))
            v.tensor_tensor(r_eq, grp, over(r_gmax, N_GROUPS), ALU.is_equal).then_inc(dve_step, 1)
            dve.wait_ge(dve_step, dve_steps.next())
            first_of(r_eq, N_GROUPS)
            v.tensor_scalar(r_om, r_eq, BIG, -BIG, ALU.mult, ALU.add).then_inc(dve_step, 1)
            dve.wait_ge(dve_step, dve_steps.next())
            for t in range(TT):
                v.tensor_tensor(r_m[:, t, :].rearrange("p (g n) -> p g n", g=N_GROUPS),
                                       exl[:, t, :].rearrange("p (g n) -> p g n", g=N_GROUPS),
                                       bc(r_om[:, t, :], [P, N_GROUPS, PER_GROUP]), ALU.add).then_inc(dve_step, 1)
                dve.wait_ge(dve_step, dve_steps.next())
            v.tensor_reduce(r_m1, r_m, AX.X, ALU.max).then_inc(dve_step, 1)
            dve.wait_ge(dve_step, dve_steps.next())
            v.tensor_tensor(r_e1, r_m, over(r_m1, N_EXP), ALU.is_equal).then_inc(dve_step, 1)
            dve.wait_ge(dve_step, dve_steps.next())
            first_of(r_e1, N_EXP)
            v.scalar_tensor_tensor(out=r_m, in0=r_e1, scalar=-2 * BIG, in1=r_m, op0=ALU.mult, op1=ALU.add).then_inc(dve_step, 1)
            dve.wait_ge(dve_step, dve_steps.next())
            v.tensor_reduce(r_m2, r_m, AX.X, ALU.max).then_inc(dve_step, 1)
            dve.wait_ge(dve_step, dve_steps.next())
            v.tensor_tensor(r_e2, r_m, over(r_m2, N_EXP), ALU.is_equal).then_inc(dve_step, 1)
            dve.wait_ge(dve_step, dve_steps.next())
            first_of(r_e2, N_EXP)
            v.tensor_tensor(r_ex, r_m2, r_m1, ALU.subtract).then_inc(sem("route_shift"), 1)
            dve.wait_ge(sem("route_shift"), done("route_shift"))
            dve.wait_ge(sem("route_exp"), 2 * l + 1)
            v.tensor_reduce(r_gsum, r_ge, AX.X, ALU.add).then_inc(dve_step, 1)
            dve.wait_ge(dve_step, dve_steps.next())
            dve.wait_ge(sem("route_exp"), 2 * l + 2)
            v.tensor_scalar(r_f, r_ex, 1.0, None, ALU.add).then_inc(dve_step, 1)
            dve.wait_ge(dve_step, dve_steps.next())
            v.tensor_tensor(r_f, r_f, r_gsum, ALU.mult).then_inc(dve_step, 1)
            dve.wait_ge(dve_step, dve_steps.next())
            v.reciprocal(r_f, r_f).then_inc(dve_step, 1)
            dve.wait_ge(dve_step, dve_steps.next())
            v.tensor_tensor(r_e2, r_e2, over(r_ex, N_EXP), ALU.mult).then_inc(dve_step, 1)
            dve.wait_ge(dve_step, dve_steps.next())
            v.tensor_tensor(r_e1, r_e1, r_e2, ALU.add).then_inc(dve_step, 1)
            dve.wait_ge(dve_step, dve_steps.next())
            v.tensor_tensor(r_gate, r_e1, over(r_f, N_EXP), ALU.mult).then_inc(sem("route_gates"), 1)
            dve.wait_ge(sem("route_gates"), done("route_gates"))

        def declare_da():
            t = tiles_of("q", 4, "act") + tiles_of("k", 4, "act") + tiles_of("v", 4, "act")
            for i in range(H):
                t += [("s", 2 * i, "dve"), ("s", 2 * i + 1, "dve")]
                if i >= 1:
                    t += [("aT", i - 1, "act")]
                if i >= 2:
                    t += [("o", i - 2, "dve")]
            t += [("aT", H - 1, "act"), ("o", H - 2, "dve"), ("o", H - 1, "dve")]
            jobs.declare("da", t + declare_head_norm("da"), EIGHT)

        da_q, da_k, da_v, da_o, da_tmp = scr(0), scr(1), scr(2), scr(3), scr(4)
        da_oT = scr(0).rearrange("p (j t) -> p j t", j=KT)
        DA_S = 3 * P
        da_mask = scr(5, DA_S)
        da_s = [scr(6, DA_S, DA_S * n) for n in range(4)]
        da_a = [scr(7, DA_S, DA_S * n) for n in range(2)]
        da_aT = [scr(7, DA_S, DA_S * (2 + n)) for n in range(2)]
        da_st = small[:, 288:288 + 16 * 8].rearrange("p (i n) -> p i n", n=8)
        da_lam = small[:, 420:430]

        def da_pe(pe, base):
            e = pe
            wait_turned(pe, 2)
            project_channels(pe, "da", "q", 4, base, hT)
            project_channels(pe, "da", "k", 4, base + 4, hT)
            project_tokens(pe, "da", "v", 4, base + 8, hT)
            q8, k8, v8 = heads(da_q), heads(da_k), da_v.rearrange("p (t h n) -> p t h n", t=TT, h=H)

            def scores(hd):
                pe.wait_ge(*taken("da", "q", hd // 2))
                pe.wait_ge(*taken("da", "k", hd // 2))
                for m in range(2):
                    pe.wait_ge(*bank_free("da", "s", 2 * hd + m))
                    bank = bank_of("da", "s", 2 * hd + m)
                    c = slice(64 * m, 64 * m + 64)
                    e.matmul(bank[:, 0:P], q8[c, hd, 0:P], k8[c, hd, 0:P], start=True, stop=True)
                    e.matmul(bank[:, P:3 * P], q8[c, hd, P:T], k8[c, hd, :], start=True, stop=True).then_inc(psum_ready, 1)

            def turn(hd):
                pe.wait_ge(sem("da_a"), hd + 1)
                pe.wait_ge(*bank_free("da", "aT", hd))
                bank = bank_of("da", "aT", hd)
                for n in range(3):
                    mm = e.transpose(bank[:, n * P:(n + 1) * P], da_a[hd % 2][:, n * P:(n + 1) * P], ident[:, :])
                mm.then_inc(psum_ready, 1)

            def pv(hd):
                pe.wait_ge(*taken("da", "aT", hd))
                if hd == 0:
                    pe.wait_ge(*taken("da", "v", 3))
                pe.wait_ge(*bank_free("da", "o", hd))
                bank = bank_of("da", "o", hd)
                a = da_aT[hd % 2]
                e.matmul(bank[:, 0:P], a[:, 0:P], v8[:, 0, hd, :], start=True, stop=True)
                e.matmul(bank[:, P:2 * P], a[:, P:2 * P], v8[:, 0, hd, :], start=True, stop=False)
                e.matmul(bank[:, P:2 * P], a[:, 2 * P:3 * P], v8[:, 1, hd, :], start=False, stop=True).then_inc(psum_ready, 1)

            for hd in range(H):
                scores(hd)
                if hd >= 1:
                    turn(hd - 1)
                if hd >= 2:
                    pv(hd - 2)
            turn(H - 1)
            pv(H - 2)
            pv(H - 1)
            o_turn_pe(pe, "da", "da", da_o)

        def da_act(act):
            a = act
            act.wait_ge(sem("da_dots"), 1)
            a.activation(da_lam[:, 2:4], da_lam[:, 0:2], ACT.Exp).then_inc(sem("da_lam_exp"), 1)
            act.wait_ge(sem("da_lam_exp"), done("da_lam_exp"))
            for name, dst in (("q", da_q), ("k", da_k)):
                for i in range(4):
                    act.wait_ge(psum_ready, job("da", name, i))
                    bank = bank_of("da", name, i)
                    a.copy(dst[:, 512 * i:512 * (i + 1)], bank).then_inc(act_took, 1)
                    act.wait_ge(act_took, act_reads.next())
            for i in range(4):
                act.wait_ge(psum_ready, job("da", "v", i))
                bank = bank_of("da", "v", i)
                a.copy(da_v.rearrange("p (t d) -> p t d", t=TT)[:, :, i * COLS:(i + 1) * COLS],
                                 bank.rearrange("p (t c) -> p t c", t=TT)).then_inc(act_took, 1)
                act.wait_ge(act_took, act_reads.next())

            def turned(hd):
                act.wait_ge(psum_ready, job("da", "aT", hd))
                bank = bank_of("da", "aT", hd)
                a.copy(da_aT[hd % 2], bank[:, 0:DA_S]).then_inc(act_took, 1)
                act.wait_ge(act_took, act_reads.next())

            for hd in range(H):
                for m in range(2):
                    i = 2 * hd + m
                    act.wait_ge(sem("da_max"), i + 1)
                    s = da_s[i % 4]
                    a.activation(s[:, 0:P], s[:, 0:P], ACT.Exp, scale=64 ** -0.5, bias=da_st[:, i, 0:1],
                                        accum_out=da_st[:, i, 2:3]).then_inc(act_step, 1)
                    act.wait_ge(act_step, act_steps.next())
                    a.activation(s[:, P:DA_S], s[:, P:DA_S], ACT.Exp, scale=64 ** -0.5, bias=da_st[:, i, 1:2],
                                         accum_out=da_st[:, i, 3:4]).then_inc(sem("da_p"), 1)
                    act.wait_ge(sem("da_p"), done("da_p"))
                if hd >= 1:
                    turned(hd - 1)
            turned(H - 1)
            head_norm_act(act, "da", st_h)
            o_turn_act(act, "da", da_oT)

        def da_dve(dve):
            v = dve
            v.tensor_tensor(lam_p[:, 0::2, :], lam_p[:, 0::2, :], lam_p[:, 1::2, :], ALU.mult).then_inc(dve_step, 1)
            dve.wait_ge(dve_step, dve_steps.next())
            v.tensor_reduce(da_lam[:, 0:2], lam_p[:, 0::2, :], AX.X, ALU.add).then_inc(sem("da_dots"), 1)
            dve.wait_ge(sem("da_dots"), done("da_dots"))
            v.memset(da_mask, 0.0).then_inc(dve_step, 1)
            dve.wait_ge(dve_step, dve_steps.next())
            for at in (0, 2 * P):
                v.tensor_scalar(da_mask[:, at:at + P], strict[:, :], -BIG, None, ALU.mult).then_inc(dve_step, 1)
                dve.wait_ge(dve_step, dve_steps.next())
            dve.wait_ge(sem("da_lam_exp"), 1)
            v.tensor_tensor(da_lam[:, 4:5], da_lam[:, 3:4], da_lam[:, 2:3], ALU.subtract).then_inc(dve_step, 1)
            dve.wait_ge(dve_step, dve_steps.next())
            v.tensor_scalar(da_lam[:, 4:5], da_lam[:, 4:5], -LAM_INIT, None, ALU.add).then_inc(dve_step, 1)
            dve.wait_ge(dve_step, dve_steps.next())

            def masked(i):
                dve.wait_ge(psum_ready, job("da", "s", i))
                bank = bank_of("da", "s", i)
                s = da_s[i % 4]
                v.tensor_tensor(s, bank[:, 0:DA_S], da_mask, ALU.add).then_inc(dve_took, 1)
                dve.wait_ge(dve_took, dve_reads.next())
                v.tensor_reduce(da_st[:, i, 0:1], s[:, 0:P], AX.X, ALU.max).then_inc(dve_step, 1)
                dve.wait_ge(dve_step, dve_steps.next())
                v.tensor_reduce(da_st[:, i, 1:2], s[:, P:DA_S], AX.X, ALU.max).then_inc(dve_step, 1)
                dve.wait_ge(dve_step, dve_steps.next())
                v.tensor_scalar(da_st[:, i, 0:2], da_st[:, i, 0:2], -(64 ** -0.5), None, ALU.mult).then_inc(sem("da_max"), 1)
                dve.wait_ge(sem("da_max"), done("da_max"))

            def mix(hd):
                i = 2 * hd
                dve.wait_ge(sem("da_p"), i + 2)
                v.reciprocal(da_st[:, i:i + 2, 4:6], da_st[:, i:i + 2, 2:4]).then_inc(dve_step, 1)
                dve.wait_ge(dve_step, dve_steps.next())
                v.tensor_scalar(da_st[:, i + 1, 4:6], da_st[:, i + 1, 4:6], da_lam[:, 4:5], None, ALU.mult).then_inc(dve_step, 1)
                dve.wait_ge(dve_step, dve_steps.next())
                s0, s1, a = da_s[i % 4], da_s[(i + 1) % 4], da_a[hd % 2]
                if hd >= 2:
                    dve.wait_ge(*taken("da", "aT", hd - 2))
                for n, x in enumerate((slice(0, P), slice(P, DA_S))):
                    v.tensor_scalar(a[:, x], s0[:, x], da_st[:, i, 4 + n:5 + n], None, ALU.mult).then_inc(dve_step, 1)
                    dve.wait_ge(dve_step, dve_steps.next())
                    last = v.scalar_tensor_tensor(out=a[:, x], in0=s1[:, x], scalar=da_st[:, i + 1, 4 + n:5 + n],
                                                  in1=a[:, x], op0=ALU.mult, op1=ALU.add)
                    if n == 0:
                        last.then_inc(dve_step, 1)
                        dve.wait_ge(dve_step, dve_steps.next())
                last.then_inc(sem("da_a"), 1)
                dve.wait_ge(sem("da_a"), done("da_a"))

            def out_of(hd):
                dve.wait_ge(psum_ready, job("da", "o", hd))
                bank = bank_of("da", "o", hd)
                o = da_o.rearrange("p (t h n) -> p t h n", t=TT, h=H)[:, :, hd, :]
                v.tensor_copy(o, bank[:, 0:T].rearrange("p (t n) -> p t n", t=TT)).then_inc(dve_took, 1)
                dve.wait_ge(dve_took, dve_reads.next())

            for hd in range(H):
                masked(2 * hd)
                masked(2 * hd + 1)
                if hd >= 1:
                    mix(hd - 1)
                if hd >= 2:
                    out_of(hd - 2)
            mix(H - 1)
            out_of(H - 2)
            out_of(H - 1)
            nw = da_norm_w[:, :].unsqueeze(1).broadcast_to([P, 16, HD])
            head_norm_dve(dve, "da", da_o, da_tmp, st_h, nw, None, RMS_EPS, 1.0 - LAM_INIT)

        HG_LN = (4, 10)
        HG_TINY = 2.0 ** -60
        hg_q, hg_k, hg_lf, hg_v, hg_g, hg_b = (scr(n) for n in range(6))
        hg_W, hg_AT, hg_mask = [scr(6), scr(8)], scr(7), scr(9)
        hg_A10, hg_o, hg_tmp = scr(2, D), scr(5), scr(6)
        hg_oT = scr(0).rearrange("p (j t) -> p j t", j=KT)
        hg_lb, hg_om = (small[:, 80 + 16 * n:96 + 16 * n].rearrange("p (o h) -> p o h", o=2) for n in range(2))
        hg_e = small[:, 320:352].rearrange("p (l h) -> p l h", l=4)
        hg_m, hg_s = small[:, 352:360], small[:, 360:368]
        N_LV = len(LEVELS)

        def declare_hg(o):
            t = []
            for name in ("f", "q", "g", "v"):
                t += tiles_of(name, 4, "act")
            t += tiles_of("d", 4, "dve") + tiles_of("lv", 4 * N_LV, "dve") + tiles_of("x10", 2, "act")
            t += tiles_of("o", 4, "dve")
            jobs.declare(f"hg{o}", t + declare_head_norm("hg"), EIGHT)

        def hg_pe(pe, o, base):
            e, key = pe, f"hg{o}"
            wait_turned(pe, HG_LN[o])
            project_channels(pe, key, "f", 4, base, hT)
            project_channels(pe, key, "q", 4, base + 4, hT)
            project_tokens(pe, key, "g", 4, base + 8, hT)
            project_tokens(pe, key, "v", 4, base + 12, hT)
            q16, k16, A16 = m16(hg_q), m16(hg_k), m16(hg_AT)
            pe.wait_ge(*taken(key, "q", 3))
            pe.wait_ge(sem("hg_k"), o + 1)
            for g in range(4):
                pe.wait_ge(*bank_free(key, "d", g))
                bank = bank_of(key, "d", g)
                for c in range(4):
                    m = 4 * g + c
                    mm = e.matmul(bank[:, c * P:(c + 1) * P], k16[:, m, :], q16[:, m, :], start=True, stop=True)
                mm.then_inc(psum_ready, 1)
            for n in range(N_LV + 1):
                pe.wait_ge(sem("hg_wq"), (N_LV + 1) * o + n + 1)
                pe.wait_ge(sem("hg_wk"), (N_LV + 1) * o + n + 1)
                if n < N_LV:
                    W16 = m16(hg_W[n % 2])
                    for g in range(4):
                        pe.wait_ge(*bank_free(key, "lv", 4 * n + g))
                        bank = bank_of(key, "lv", 4 * n + g)
                        for c in range(4):
                            m = 4 * g + c
                            mm = e.matmul(bank[:, c * P:(c + 1) * P], W16[:, m, :], W16[:, m, :], start=True, stop=True)
                        mm.then_inc(psum_ready, 1)
                else:
                    W8 = heads(hg_W[n % 2])
                    for g in range(2):
                        pe.wait_ge(*bank_free(key, "x10", g))
                        bank = bank_of(key, "x10", g)
                        for c in range(4):
                            mm = e.matmul(bank[:, c * P:(c + 1) * P], W8[:, 4 * g + c, 0:P], W8[:, 4 * g + c, P:T],
                                          start=True, stop=True)
                        mm.then_inc(psum_ready, 1)
            v8, x8 = hg_v.rearrange("p (t h n) -> p t h n", t=TT, h=H), heads(hg_A10)
            pe.wait_ge(*taken(key, "v", 3))
            pe.wait_ge(*taken(key, "lv", 4 * N_LV - 1))
            for i in range(4):
                if i == 2:
                    pe.wait_ge(*taken(key, "x10", 1))
                pe.wait_ge(*bank_free(key, "o", i))
                bank = bank_of(key, "o", i)
                for c in range(4):
                    hd = 4 * (i % 2) + c
                    dst = bank[:, c * P:(c + 1) * P]
                    if i < 2:
                        mm = e.matmul(dst, A16[:, 2 * hd, :], v8[:, 0, hd, :], start=True, stop=True)
                    else:
                        e.matmul(dst, x8[:, hd, :], v8[:, 0, hd, :], start=True, stop=False)
                        mm = e.matmul(dst, A16[:, 2 * hd + 1, :], v8[:, 1, hd, :], start=False, stop=True)
                mm.then_inc(psum_ready, 1)
            o_turn_pe(pe, key, "hg", hg_o, o + 1)

        def hg_act(act, o):
            a, key = act, f"hg{o}"
            if o == 0:
                act.wait_ge(sem("hg_lb_shift"), 1)
                a.activation(hg_e, hg_e, ACT.Exp).then_inc(sem("hg_lb_exp"), 1)
                act.wait_ge(sem("hg_lb_exp"), done("hg_lb_exp"))
            for i in range(4):
                act.wait_ge(psum_ready, job(key, "f", i))
                bank = bank_of(key, "f", i)
                x = slice(512 * i, 512 * (i + 1))
                a.activation(hg_lf[:, x], bank, ACT.Sigmoid).then_inc(act_step, 1)
                act.wait_ge(act_step, act_steps.next())
                a.activation(hg_k[:, x], bank, ACT.Sigmoid, scale=-1.0).then_inc(act_step, 1)
                act.wait_ge(act_step, act_steps.next())
                a.copy(hg_b[:, x], bank).then_inc(act_took, 1)
                act.wait_ge(act_took, act_reads.next())
            for i in range(4):
                act.wait_ge(psum_ready, job(key, "q", i))
                bank = bank_of(key, "q", i)
                a.activation(hg_q[:, 512 * i:512 * (i + 1)], bank, ACT.Silu).then_inc(act_took, 1)
                act.wait_ge(act_took, act_reads.next())
            act.wait_ge(sem("hg_arg"), o + 1)
            a.activation(hg_lf, hg_lf, ACT.Ln).then_inc(sem("hg_log"), 1)
            act.wait_ge(sem("hg_log"), done("hg_log"))
            for name, dst, f in (("g", hg_g, ACT.Silu), ("v", hg_v, ACT.Copy)):
                for i in range(4):
                    act.wait_ge(psum_ready, job(key, name, i))
                    bank = bank_of(key, name, i)
                    a.activation(dst.rearrange("p (t d) -> p t d", t=TT)[:, :, i * COLS:(i + 1) * COLS],
                                           bank.rearrange("p (t c) -> p t c", t=TT), f).then_inc(act_took, 1)
                    act.wait_ge(act_took, act_reads.next())
            for n in range(N_LV + 1):
                act.wait_ge(sem("hg_shift"), (N_LV + 1) * o + n + 1)
                a.activation(hg_W[n % 2], hg_W[n % 2], ACT.Exp).then_inc(sem("hg_exp"), 1)
                act.wait_ge(sem("hg_exp"), done("hg_exp"))
            for i in range(2):
                act.wait_ge(psum_ready, job(key, "x10", i))
                bank = bank_of(key, "x10", i)
                a.copy(hg_A10[:, 512 * i:512 * (i + 1)], bank).then_inc(act_took, 1)
                act.wait_ge(act_took, act_reads.next())
            head_norm_act(act, "hg", st_h, o + 1)
            o_turn_act(act, key, hg_oT)

        def hg_pool(pool, o):
            g = pool
            for n in range(N_LV + 1):
                pool.wait_ge(sem("hg_exp"), (N_LV + 1) * o + n + 1)
                if n == 0:
                    pool.wait_ge(*taken(f"hg{o}", "q", 3))
                m = 1 << n
                w, q = (x.rearrange("p (b f r) -> p b f r", f=2, r=m)[:, :, 1, :] for x in (hg_W[n % 2], hg_q))
                g.tensor_tensor(w, w, q, ALU.mult).then_inc(sem("hg_wq"), 1)
                pool.wait_ge(sem("hg_wq"), done("hg_wq"))

        def hg_dve(dve, o):
            v, key = dve, f"hg{o}"
            if o == 0:
                lt = lb_log.rearrange("p l h -> p h l")
                v.tensor_reduce(hg_m, lt, AX.X, ALU.max).then_inc(dve_step, 1)
                dve.wait_ge(dve_step, dve_steps.next())
                v.tensor_tensor(hg_e, lb_log, hg_m.unsqueeze(1).broadcast_to([P, 4, H]), ALU.subtract).then_inc(sem("hg_lb_shift"), 1)
                dve.wait_ge(sem("hg_lb_shift"), done("hg_lb_shift"))
                dve.wait_ge(sem("hg_lb_exp"), 1)
                v.tensor_reduce(hg_s, hg_e.rearrange("p l h -> p h l"), AX.X, ALU.add).then_inc(dve_step, 1)
                dve.wait_ge(dve_step, dve_steps.next())
                v.reciprocal(hg_s, hg_s).then_inc(dve_step, 1)
                dve.wait_ge(dve_step, dve_steps.next())
                v.tensor_tensor(hg_e, hg_e, hg_s.unsqueeze(1).broadcast_to([P, 4, H]), ALU.mult).then_inc(dve_step, 1)
                dve.wait_ge(dve_step, dve_steps.next())
                v.memset(hg_lb[:, 0, :], 0.0).then_inc(dve_step, 1)
                dve.wait_ge(dve_step, dve_steps.next())
                v.tensor_tensor(hg_lb[:, 1, :], hg_e[:, 1, :], hg_e[:, 2, :], ALU.add).then_inc(dve_step, 1)
                dve.wait_ge(dve_step, dve_steps.next())
                v.tensor_tensor(hg_lb[:, 1, :], hg_lb[:, 1, :], hg_e[:, 3, :], ALU.add).then_inc(dve_step, 1)
                dve.wait_ge(dve_step, dve_steps.next())
                v.tensor_scalar(hg_om, hg_lb, -1.0, 1.0, ALU.mult, ALU.add).then_inc(dve_step, 1)
                dve.wait_ge(dve_step, dve_steps.next())
            dve.wait_ge(*taken(key, "f", 3))
            for hd in range(H):
                x = slice(T * hd, T * (hd + 1))
                v.tensor_scalar(hg_lf[:, x], hg_lf[:, x], hg_om[:, o, hd:hd + 1], hg_lb[:, o, hd:hd + 1],
                                       ALU.mult, ALU.add).then_inc(dve_step, 1)
                dve.wait_ge(dve_step, dve_steps.next())
            v.tensor_scalar(hg_mask, hg_lf, HG_TINY, None, ALU.is_lt).then_inc(dve_step, 1)
            dve.wait_ge(dve_step, dve_steps.next())
            v.tensor_scalar(hg_lf, hg_lf, HG_TINY, None, ALU.max).then_inc(sem("hg_arg"), 1)
            dve.wait_ge(sem("hg_arg"), done("hg_arg"))
            for hd in range(H):
                x = slice(T * hd, T * (hd + 1))
                last = v.tensor_scalar(hg_k[:, x], hg_k[:, x], hg_om[:, o, hd:hd + 1], None, ALU.mult)
                if hd < H - 1:
                    last.then_inc(dve_step, 1)
                    dve.wait_ge(dve_step, dve_steps.next())
            last.then_inc(sem("hg_k"), 1)
            dve.wait_ge(sem("hg_k"), done("hg_k"))
            dve.wait_ge(sem("hg_log"), o + 1)
            v.copy_predicated(hg_lf, hg_mask.bitcast(I32), hg_b).then_inc(dve_step, 1)
            dve.wait_ge(dve_step, dve_steps.next())
            v.memset(hg_mask, 1.0).then_inc(dve_step, 1)
            dve.wait_ge(dve_step, dve_steps.next())
            v.memset(hg_mask.rearrange("p (b r) -> p b r", r=64)[:, :, 0:1], 0.0).then_inc(dve_step, 1)
            dve.wait_ge(dve_step, dve_steps.next())
            v.tensor_tensor_scan(hg_b, hg_mask, hg_lf, 0.0, ALU.mult, ALU.add).then_inc(dve_step, 1)
            dve.wait_ge(dve_step, dve_steps.next())

            def exponents(n):
                m = 1 << n
                if n >= 2:
                    dve.wait_ge(psum_ready, job(key, "lv", 4 * (n - 2) + 3))
                W = hg_W[n % 2]
                if n < N_LV:
                    nb = UNIT // (2 * m)
                    w, b = (x.rearrange("p (b f r) -> p b f r", f=2, r=m) for x in (W, hg_b))
                    ref = b[:, :, 0, m - 1:m].broadcast_to([P, nb, m])
                    if m < 64:
                        v.tensor_tensor(w[:, :, 1, :], b[:, :, 1, :], ref, ALU.subtract).then_inc(dve_step, 1)
                        dve.wait_ge(dve_step, dve_steps.next())
                    else:
                        v.tensor_copy(w[:, :, 1, :], b[:, :, 1, :]).then_inc(dve_step, 1)
                        dve.wait_ge(dve_step, dve_steps.next())
                    v.tensor_tensor(w[:, :, 0, :], ref, b[:, :, 0, :], ALU.subtract).then_inc(sem("hg_shift"), 1)
                    dve.wait_ge(sem("hg_shift"), done("hg_shift"))
                    return
                w, b = (x.rearrange("p (h c r) -> p h c r", h=H, c=4) for x in (W, hg_b))
                end = lambda c: b[:, :, c, 63:64].broadcast_to([P, H, 64])
                v.tensor_copy(w[:, :, 2, :], b[:, :, 2, :]).then_inc(dve_step, 1)
                dve.wait_ge(dve_step, dve_steps.next())
                v.tensor_tensor(w[:, :, 3, :], b[:, :, 3, :], end(2), ALU.add).then_inc(dve_step, 1)
                dve.wait_ge(dve_step, dve_steps.next())
                v.tensor_tensor(w[:, :, 1, :], end(1), b[:, :, 1, :], ALU.subtract).then_inc(dve_step, 1)
                dve.wait_ge(dve_step, dve_steps.next())
                v.tensor_tensor(w[:, :, 0, :], end(0), b[:, :, 0, :], ALU.subtract).then_inc(dve_step, 1)
                dve.wait_ge(dve_step, dve_steps.next())
                v.tensor_tensor(w[:, :, 0, :], w[:, :, 0, :], end(1), ALU.add).then_inc(sem("hg_shift"), 1)
                dve.wait_ge(sem("hg_shift"), done("hg_shift"))

            def k_part(n):
                m = 1 << n
                dve.wait_ge(sem("hg_exp"), (N_LV + 1) * o + n + 1)
                w, k = (x.rearrange("p (b f r) -> p b f r", f=2, r=m)[:, :, 0, :] for x in (hg_W[n % 2], hg_k))
                v.tensor_tensor(w, w, k, ALU.mult).then_inc(sem("hg_wk"), 1)
                dve.wait_ge(sem("hg_wk"), done("hg_wk"))

            A16 = m16(hg_AT)
            exponents(0)
            for g in range(4):
                dve.wait_ge(psum_ready, job(key, "d", g))
                bank = bank_of(key, "d", g)
                v.tensor_tensor(A16[:, 4 * g:4 * g + 4, :], bank.rearrange("p (c n) -> p c n", c=4),
                                          ident[:, :].unsqueeze(1).broadcast_to([P, 4, P]), ALU.mult).then_inc(dve_took, 1)
                dve.wait_ge(dve_took, dve_reads.next())
            for n in range(N_LV):
                exponents(n + 1)
                k_part(n)
                pick = level[:, n, :].bitcast(I16).unsqueeze(1).broadcast_to([P, 4, P])
                for g in range(4):
                    dve.wait_ge(psum_ready, job(key, "lv", 4 * n + g))
                    bank = bank_of(key, "lv", 4 * n + g)
                    v.copy_predicated(A16[:, 4 * g:4 * g + 4, :], pick, bank.rearrange("p (c n) -> p c n", c=4)).then_inc(dve_took, 1)
                    dve.wait_ge(dve_took, dve_reads.next())
            k_part(N_LV)
            for i in range(4):
                dve.wait_ge(psum_ready, job(key, "o", i))
                bank = bank_of(key, "o", i)
                v.tensor_copy(hg_o[:, 512 * i:512 * (i + 1)], bank).then_inc(dve_took, 1)
                dve.wait_ge(dve_took, dve_reads.next())
            nw = hg_norm_w[:, o, :].unsqueeze(1).broadcast_to([P, 16, HD])
            head_norm_dve(dve, "hg", hg_o, hg_tmp, st_h, nw, hg_g, RMS_EPS)

        ML_TURN = 6
        ml_q, ml_k = scr(0, D), scr(0, D, D)
        ml_v = scr(1, TT * H * (HD + 1)).rearrange("p (t h n) -> p t h n", t=TT, h=H)
        ml_w, ml_g = scr(2, D, 512), scr(3)
        ML_S = 3 * P
        ml_D = scr(4, H * ML_S).rearrange("p (h n) -> p h n", h=H)
        ml_S = scr(6, H * ML_S).rearrange("p (h n) -> p h n", h=H)
        ml_row = [scr(7, T, D + T * n)[0:H, :] for n in range(4)]
        ml_pad = [scr(8, 2 * 260), scr(8, 2 * 260, 520)]
        ml_o, ml_tmp = scr(5), scr(4)
        ml_oT = scr(0).rearrange("p (j t) -> p j t", j=KT)
        ml_aT, ml_em = (th(small[:, 288 + 16 * n:304 + 16 * n]) for n in range(2))
        ml_den = small[:, 320:336].rearrange("p (i n) -> p i n", n=2)

        def declare_ml():
            t = tiles_of("gate", 1, "dve") + tiles_of("qk", 4, "act") + tiles_of("og", 4, "act") + tiles_of("v", 4, "act")
            t += tiles_of("aT", 1, "dve") + tiles_of("M", 4, "dve")
            t += tiles_of("s", 8, "dve") + tiles_of("o", 8, "dve")
            jobs.declare("ml", t + declare_head_norm("ml"), EIGHT)

        def ml_pe(pe, base):
            e = pe
            wait_turned(pe, ML_TURN)
            pe.wait_ge(*bank_free("ml", "gate"))
            bank = bank_of("ml", "gate")
            for n in range(2):
                for j in range(KT):
                    mm = e.matmul(bank[0:H, n * T:(n + 1) * T], ml_gate_w[:, j, n * H:(n + 1) * H], hT[:, j, :],
                                  start=(j == 0), stop=(j == KT - 1))
            mm.then_inc(psum_ready, 1)
            project_channels(pe, "ml", "qk", 4, base, hT)
            project_tokens(pe, "ml", "og", 4, base + 4, hT)
            project_tokens(pe, "ml", "v", 4, base + 8, hT)
            pe.wait_ge(sem("ml_rows"), 1)
            pe.wait_ge(*bank_free("ml", "aT"))
            bank = bank_of("ml", "aT")
            for n, row in enumerate((0, 1)):
                for t in range(TT):
                    mm = e.transpose(bank[:, (2 * n + t) * H:(2 * n + t + 1) * H], ml_row[row][:, t * P:(t + 1) * P],
                                     ident[0:H, 0:H])
            mm.then_inc(psum_ready, 1)
            for i in range(4):
                pe.wait_ge(*bank_free("ml", "M", i))
                bank = bank_of("ml", "M", i)
                for c in range(2):
                    hd = 2 * i + c
                    mm = e.matmul(bank[:, c * T:(c + 1) * T], ident[0:H, hd:hd + 1].broadcast_to([H, P]), ml_row[3],
                                  start=True, stop=True)
                mm.then_inc(psum_ready, 1)
            pe.wait_ge(sem("ml_silu"), 2)
            pe.wait_ge(sem("ml_k"), 4)
            for hd in range(H):
                pe.wait_ge(*bank_free("ml", "s", hd))
                bank = bank_of("ml", "s", hd)
                c, half = slice(T * (hd // 2), T * (hd // 2 + 1)), slice(64 * (hd % 2), 64 * (hd % 2) + 64)
                k, q = ml_k[half, c], ml_q[half, c]
                e.matmul(bank[:, 0:T], k[:, 0:P], q, start=True, stop=True)
                e.matmul(bank[:, T:ML_S], k[:, P:T], q[:, P:T], start=True, stop=True).then_inc(psum_ready, 1)
            pe.wait_ge(*taken("ml", "v", 3))
            pe.wait_ge(sem("ml_ones"), 1)
            for i in range(8):
                t = i // 4
                if i == 0:
                    pe.wait_ge(*taken("ml", "s", H - 1))
                pe.wait_ge(*bank_free("ml", "o", i))
                bank = bank_of("ml", "o", i)
                for c in range(2):
                    hd = 2 * (i % 4) + c
                    dst = bank[:, c * (HD + 1):(c + 1) * (HD + 1)]
                    if t == 0:
                        mm = e.matmul(dst, ml_S[:, hd, 0:P], ml_v[:, 0, hd, :], start=True, stop=True)
                    else:
                        e.matmul(dst, ml_S[:, hd, P:T], ml_v[:, 0, hd, :], start=True, stop=False)
                        mm = e.matmul(dst, ml_S[:, hd, T:ML_S], ml_v[:, 1, hd, :], start=False, stop=True)
                mm.then_inc(psum_ready, 1)
            o_turn_pe(pe, "ml", "ml", ml_o)

        def ml_act(act):
            a = act
            act.wait_ge(sem("ml_abs"), 1)
            a.activation(ml_row[3], ml_row[3], ACT.Exp, scale=-1.0).then_inc(act_step, 1)
            act.wait_ge(act_step, act_steps.next())
            a.activation(ml_row[3], ml_row[3], ACT.Ln, bias=1.0).then_inc(sem("ml_log"), 1)
            act.wait_ge(sem("ml_log"), done("ml_log"))
            for i in range(4):
                act.wait_ge(psum_ready, job("ml", "qk", i))
                bank = bank_of("ml", "qk", i)
                if i == 0:
                    act.wait_ge(sem("ml_pad_zero"), 1)
                if i >= 2:
                    act.wait_ge(sem("ml_conv"), 2 * (i - 1))
                a.copy(ml_pad[i % 2].rearrange("p (c n) -> p c n", c=2)[:, :, 3:3 + T],
                                 bank.rearrange("p (c n) -> p c n", c=2)).then_inc(act_took, 1)
                act.wait_ge(act_took, act_reads.next())
                if i >= 1:
                    ml_silu(act, i - 1)
            ml_silu(act, 3)
            for name, f in (("og", ACT.Sigmoid), ("v", ACT.Copy)):
                for i in range(4):
                    act.wait_ge(psum_ready, job("ml", name, i))
                    bank = bank_of("ml", name, i)
                    if name == "og":
                        a.activation(ml_g.rearrange("p (t d) -> p t d", t=TT)[:, :, i * COLS:(i + 1) * COLS],
                                               bank.rearrange("p (t c) -> p t c", t=TT), f).then_inc(act_took, 1)
                        act.wait_ge(act_took, act_reads.next())
                    else:
                        b4 = bank.rearrange("p (t h n) -> p t h n", t=TT, h=2)
                        for t in range(TT):
                            last = a.copy(ml_v[:, t, 2 * i:2 * i + 2, 0:HD], b4[:, t, :, :])
                        last.then_inc(act_took, 1)
                        act.wait_ge(act_took, act_reads.next())
            act.wait_ge(*taken("ml", "aT"))
            a.activation(ml_em, ml_em, ACT.Exp, scale=-1.0).then_inc(sem("ml_em_exp"), 1)
            act.wait_ge(sem("ml_em_exp"), done("ml_em_exp"))
            act.wait_ge(*taken("ml", "M", 3))
            a.activation(ml_D, ml_D, ACT.Exp, scale=-1.0).then_inc(sem("ml_D_exp"), 1)
            act.wait_ge(sem("ml_D_exp"), done("ml_D_exp"))
            head_norm_act(act, "ml", st_h)
            o_turn_act(act, "ml", ml_oT)

        def ml_silu(act, i):
            act.wait_ge(sem("ml_conv"), 2 * (i + 1))
            x = (ml_q, ml_k)[i // 2][:, 512 * (i % 2):512 * (i % 2 + 1)]
            act.activation(x, x, ACT.Silu).then_inc(sem("ml_silu"), 1)
            act.wait_ge(sem("ml_silu"), done("ml_silu"))

        def ml_pool(pool):
            g = pool
            pool.wait_ge(sem("ln_done"), 2 * ML_TURN)
            g.dma_start(ml_w, W["mlstm_norm_w_2"][0].partition_broadcast(P)).then_inc(sem("ml_w_landed"), 16)
            g.memset(ml_v[:, 0, :, HD:], 1.0).then_inc(pool_step, 1)
            pool.wait_ge(pool_step, pool_steps.next())
            g.memset(ml_v[:, 1, :, HD:], 1.0).then_inc(sem("ml_ones"), 1)
            pool.wait_ge(sem("ml_ones"), done("ml_ones"))
            pool.wait_ge(sem("ml_w_landed"), 16)
            pool.wait_ge(*taken("ml", "og", 3))
            g3 = ml_g.rearrange("p (t d) -> p t d", t=TT)
            g.tensor_tensor(g3, g3, ml_w.unsqueeze(1).broadcast_to([P, TT, D]), ALU.mult).then_inc(sem("ml_gate"), 1)
            pool.wait_ge(sem("ml_gate"), done("ml_gate"))

        def ml_dve(dve):
            v = dve
            for b in range(2):
                last = v.memset(ml_pad[b].rearrange("p (c n) -> p c n", c=2)[:, :, 0:3], 0.0)
                if b == 0:
                    last.then_inc(dve_step, 1)
                    dve.wait_ge(dve_step, dve_steps.next())
            last.then_inc(sem("ml_pad_zero"), 1)
            dve.wait_ge(sem("ml_pad_zero"), done("ml_pad_zero"))
            r_i, r_f, r_b, r_x = ml_row
            dve.wait_ge(psum_ready, job("ml", "gate"))
            bank = bank_of("ml", "gate")
            v.tensor_scalar(r_i, bank[0:H, 0:T], ml_gate_b[:, 0:1], None, ALU.add).then_inc(dve_step, 1)
            dve.wait_ge(dve_step, dve_steps.next())
            v.tensor_scalar(r_f, bank[0:H, T:2 * T], ml_gate_b[:, 1:2], None, ALU.add).then_inc(dve_took, 1)
            dve.wait_ge(dve_took, dve_reads.next())
            magnitude(v, r_x, r_f).then_inc(sem("ml_abs"), 1)
            dve.wait_ge(sem("ml_abs"), done("ml_abs"))
            dve.wait_ge(sem("ml_log"), 1)
            v.tensor_scalar(r_f, r_f, 0.0, None, ALU.min).then_inc(dve_step, 1)
            dve.wait_ge(dve_step, dve_steps.next())
            v.tensor_tensor(r_f, r_f, r_x, ALU.subtract).then_inc(dve_step, 1)
            dve.wait_ge(dve_step, dve_steps.next())
            v.tensor_tensor_scan(r_b, ones[0:H, 0:1].broadcast_to([H, T]), r_f, 0.0, ALU.mult, ALU.add).then_inc(dve_step, 1)
            dve.wait_ge(dve_step, dve_steps.next())
            v.tensor_tensor(r_i, r_i, r_b, ALU.subtract).then_inc(dve_step, 1)
            dve.wait_ge(dve_step, dve_steps.next())
            v.tensor_tensor_scan(r_x, r_i, r_i, 0.0, ALU.max, ALU.max).then_inc(dve_step, 1)
            dve.wait_ge(dve_step, dve_steps.next())
            v.tensor_tensor(r_f, r_b, r_x, ALU.add).then_inc(sem("ml_rows"), 1)
            dve.wait_ge(sem("ml_rows"), done("ml_rows"))
            for i in range(4):
                dve.wait_ge(*taken("ml", "qk", i))
                p = ml_pad[i % 2].rearrange("p (c n) -> p c n", c=2)
                for c in range(2):
                    ch = 2 * i + c
                    dst = (ml_q, ml_k)[i // 2][:, T * (ch % 4):T * (ch % 4 + 1)]
                    conv_silu(dve, p[:, c, :], dst, [conv_m[:, k, ch:ch + 1] for k in range(CONV)]).then_inc(sem("ml_conv"), 1)
                    dve.wait_ge(sem("ml_conv"), done("ml_conv"))
            for i in range(4):
                x = ml_k[:, T * i:T * (i + 1)]
                dve.wait_ge(sem("ml_silu"), 2 + i // 2 + 1)
                v.tensor_scalar(x, x, 64 ** -0.5, None, ALU.mult).then_inc(sem("ml_k"), 1)
                dve.wait_ge(sem("ml_k"), done("ml_k"))
            dve.wait_ge(psum_ready, job("ml", "aT"))
            bank = bank_of("ml", "aT")
            v.tensor_copy(ml_aT, th(bank[:, 0:2 * H])).then_inc(dve_step, 1)
            dve.wait_ge(dve_step, dve_steps.next())
            v.tensor_copy(ml_em, th(bank[:, 2 * H:4 * H])).then_inc(dve_took, 1)
            dve.wait_ge(dve_took, dve_reads.next())
            for i in range(4):
                dve.wait_ge(psum_ready, job("ml", "M", i))
                bank = bank_of("ml", "M", i)
                for c in range(2):
                    hd = 2 * i + c
                    v.tensor_scalar(ml_D[:, hd, 0:T], bank[:, c * T:(c + 1) * T], ml_aT[:, 0, hd:hd + 1], 0.0,
                                           ALU.subtract, ALU.max).then_inc(dve_step, 1)
                    dve.wait_ge(dve_step, dve_steps.next())
                    last = v.tensor_scalar(ml_D[:, hd, T:ML_S], bank[:, c * T + P:(c + 1) * T], ml_aT[:, 1, hd:hd + 1],
                                           0.0, ALU.subtract, ALU.max)
                    if c == 0:
                        last.then_inc(dve_step, 1)
                        dve.wait_ge(dve_step, dve_steps.next())
                last.then_inc(dve_took, 1)
                dve.wait_ge(dve_took, dve_reads.next())
            dve.wait_ge(sem("ml_D_exp"), 1)
            diag = ml_D.rearrange("p h (a n) -> p h a n", a=3)
            for n in (0, 2):
                v.tensor_tensor(diag[:, :, n, :], diag[:, :, n, :],
                                       causal[:, :].unsqueeze(1).broadcast_to([P, H, P]), ALU.mult).then_inc(dve_step, 1)
                dve.wait_ge(dve_step, dve_steps.next())
            for hd in range(H):
                dve.wait_ge(psum_ready, job("ml", "s", hd))
                bank = bank_of("ml", "s", hd)
                v.tensor_tensor(ml_S[:, hd, :], bank[:, 0:ML_S], ml_D[:, hd, :], ALU.mult).then_inc(dve_took, 1)
                dve.wait_ge(dve_took, dve_reads.next())
            dve.wait_ge(sem("ml_em_exp"), 1)
            o4 = ml_o.rearrange("p (t h n) -> p t h n", t=TT, h=H)
            for i in range(8):
                t, hs = i // 4, slice(2 * (i % 4), 2 * (i % 4) + 2)
                dve.wait_ge(psum_ready, job("ml", "o", i))
                bank = bank_of("ml", "o", i)[:, 0:2 * (HD + 1)].rearrange("p (c n) -> p c n", c=2)
                den = ml_den[:, i, :]
                v.tensor_copy(den, bank[:, :, HD]).then_inc(dve_step, 1)
                dve.wait_ge(dve_step, dve_steps.next())
                magnitude(v, den, den).then_inc(dve_step, 1)
                dve.wait_ge(dve_step, dve_steps.next())
                v.tensor_tensor(den, den, ml_em[:, t, hs], ALU.max).then_inc(dve_step, 1)
                dve.wait_ge(dve_step, dve_steps.next())
                v.reciprocal(den, den).then_inc(dve_step, 1)
                dve.wait_ge(dve_step, dve_steps.next())
                v.tensor_tensor(o4[:, t, hs, :], bank[:, :, 0:HD], bc(den, [P, 2, HD]), ALU.mult).then_inc(dve_took, 1)
                dve.wait_ge(dve_took, dve_reads.next())
            dve.wait_ge(sem("ml_gate"), 1)
            head_norm_dve(dve, "ml", ml_o, ml_tmp, st_h, None, ml_g, RMS_EPS)

        S5_TURN = 8
        QT = 4
        MAGIC = 1.5 * 2.0 ** 23
        TWO_PI = (6.28125, 0.0019350051879882812, 2 * math.pi - 6.28125 - 0.0019350051879882812)
        PI_BELOW = 3.141592
        s5_u, s5_BT, s5_CT, s5_y = scr(0), m16(scr(1)), m16(scr(2)), scr(3)
        s5_bst = scr(3).rearrange("p (r j g c) -> p r j g c", r=2, j=S5_TILES, g=2)
        s5_braw = scr(4, 1024).rearrange("p (r j c) -> p r j c", r=2, c=S5_C)
        s5_craw = scr(4, 1024, 1024).rearrange("p (r q n) -> p r q n", r=2, n=S5_N)
        s5_cst = scr(5).rearrange("p (r q n) -> p r q n", r=2, n=P)
        s5_t = scr(6, 2 * S5_TILES * S5_C).rearrange("p (r j c) -> p r j c", r=2, c=S5_C)

        def quad(x):
            return x.rearrange("p (r a t) -> p r a t", r=2, a=QT)
        s5_tab = [quad(scr(4)), quad(scr(5))]
        s5_w, s5_g, s5_x = quad(scr(6)), quad(scr(7)), [quad(scr(8)), quad(scr(9))]
        s5_oT = scr(3).rearrange("p (j t) -> p j t", j=KT)
        s5_sg, s5_mix = (scr(n).rearrange("p (t d) -> p t d", t=TT) for n in (1, 6))
        names = ("dt", "mag", "th", "n", "r", "sin", "half", "den", "cr", "ci", "tmp", "nr")
        s5 = {k: small[:, 288 + 32 * i:320 + 32 * i] for i, k in enumerate(names)}
        s5_parity = small[:, 700:702]
        s5_pow = sb("s5_pow", [P, 2, 8, S5_TILES])
        s5_ldt = small[:, 704:704 + S5_G]
        s5_pt = hT[:, 0:4, :].rearrange("p (r a) (b t) -> p r (a b) t", r=2, b=2)

        def declare_s5():
            t = tiles_of("u", 4, "act") + tiles_of("bT", 4, "act") + tiles_of("cT", 4, "act")
            for q in range(KT):
                t += [("bu", QT * q + j, "dve") for j in range(QT)]
                if q >= 1:
                    t += [("y", q - 1, "dve")]
            t += [("y", KT - 1, "dve")] + tiles_of("zb", 4, "act")
            jobs.declare("s5", t, FOUR)

        def s5_pe(pe, base):
            e = pe
            wait_turned(pe, S5_TURN)
            project_channels(pe, "s5", "u", 4, base, hT)
            b16 = scr(3).rearrange("p (m n) -> p m n", n=P)
            c16 = scr(5).rearrange("p (m n) -> p m n", n=P)
            for name, src in (("bT", b16), ("cT", c16)):
                pe.wait_ge(sem("s5_" + name), 1)
                for i in range(4):
                    pe.wait_ge(*bank_free("s5", name, i))
                    bank = bank_of("s5", name, i)
                    for c in range(4):
                        mm = e.transpose(bank[:, c * P:(c + 1) * P], src[:, 4 * i + c, :], ident[:, :])
                    mm.then_inc(psum_ready, 1)
            u8 = heads(s5_u)
            for i in range(4):
                pe.wait_ge(*taken("s5", "u", i))
            pe.wait_ge(*taken("s5", "cT", 3))

            def y_of(q):
                pe.wait_ge(sem("s5_x"), q + 1)
                pe.wait_ge(*bank_free("s5", "y", q))
                bank = bank_of("s5", "y", q)
                x = s5_x[q % 2]
                for j in range(QT):
                    rows_ = slice(32 * j, 32 * j + 32)
                    for r in range(2):
                        mm = e.matmul(bank[rows_, 0:T], s5_CT[:, r * KT + q, rows_], x[:, r, j, :],
                                      start=(r == 0), stop=(r == 1))
                mm.then_inc(psum_ready, 1)

            for q in range(KT):
                for j in range(QT):
                    pe.wait_ge(*bank_free("s5", "bu", QT * q + j))
                    bank = bank_of("s5", "bu", QT * q + j)
                    rows_ = slice(32 * j, 32 * j + 32)
                    for r in range(2):
                        mm = e.matmul(bank[:, r * T:(r + 1) * T], s5_BT[rows_, r * KT + q, :], u8[rows_, q, :],
                                      start=True, stop=True)
                    mm.then_inc(psum_ready, 1)
                if q >= 1:
                    y_of(q - 1)
            y_of(KT - 1)
            pe.wait_ge(sem("s5_gelu"), KT)

        def s5_act(act):
            a = act
            act.wait_ge(sem("s5_ldt"), 1)
            a.activation(s5["dt"], s5["dt"], ACT.Exp).then_inc(sem("s5_dt"), 1)
            act.wait_ge(sem("s5_dt"), done("s5_dt"))
            act.wait_ge(sem("s5_re_dt"), 1)
            a.activation(s5["mag"], s5["tmp"], ACT.Exp).then_inc(act_step, 1)
            act.wait_ge(act_step, act_steps.next())
            a.activation(s5["sin"], s5["r"], ACT.Sin).then_inc(act_step, 1)
            act.wait_ge(act_step, act_steps.next())
            a.activation(s5["half"], s5["r"], ACT.Sin, scale=0.5).then_inc(sem("s5_sin"), 1)
            act.wait_ge(sem("s5_sin"), done("s5_sin"))
            for i in range(4):
                act.wait_ge(psum_ready, job("s5", "u", i))
                bank = bank_of("s5", "u", i)
                a.copy(s5_u[:, 512 * i:512 * (i + 1)], bank).then_inc(act_took, 1)
                act.wait_ge(act_took, act_reads.next())
            for name, dst in (("bT", s5_BT), ("cT", s5_CT)):
                for i in range(4):
                    act.wait_ge(psum_ready, job("s5", name, i))
                    bank = bank_of("s5", name, i)
                    a.copy(dst[:, 4 * i:4 * i + 4, :], bank.rearrange("p (c n) -> p c n", c=4)).then_inc(act_took, 1)
                    act.wait_ge(act_took, act_reads.next())
            for q in range(KT):
                act.wait_ge(*taken("s5", "y", q))
                x = s5_y[:, T * q:T * (q + 1)]
                a.activation(x, x, ACT.Gelu_apprx_tanh).then_inc(sem("s5_gelu"), 1)
                act.wait_ge(sem("s5_gelu"), done("s5_gelu"))
            for i in range(4):
                act.wait_ge(psum_ready, job("s5", "zb", i))
                bank = bank_of("s5", "zb", i)
                a.activation(s5_sg[:, :, i * COLS:(i + 1) * COLS], bank.rearrange("p (t c) -> p t c", t=TT),
                                       ACT.Sigmoid).then_inc(act_took, 1)
                act.wait_ge(act_took, act_reads.next())

        def s5_pool(pool):
            g = pool
            pool.wait_ge(sem("ln_done"), 2 * S5_TURN)
            g.dma_start(s5_ldt[:, :], W["s5_log_dt_2"][0].partition_broadcast(P)).then_inc(sem("s5_landed"), 16)
            for r, (b, c) in enumerate((("s5_b_re_2", "s5_c_re_2"), ("s5_b_im_2", "s5_c_im_2"))):
                g.dma_start(s5_braw[:, r, :, :], W[b][0].rearrange("(j g) p c -> (g p) j c", g=2))\
                    .then_inc(sem("s5_landed"), 16)
                g.dma_start(s5_craw[:, r, :, :], W[c][0].rearrange("(q g) c p -> (g c) q p", g=KT))\
                    .then_inc(sem("s5_landed"), 16)
            pool.wait_ge(sem("s5_pow"), 1)
            pool.wait_ge(*taken("s5", "cT", 3))
            for q in range(KT):
                if q >= 2:
                    pool.wait_ge(sem("s5_x"), q - 1)
                tab = s5_tab[q % 2]
                g.memset(tab[:, 0, :, 0:1], 1.0).then_inc(pool_step, 1)
                pool.wait_ge(pool_step, pool_steps.next())
                g.memset(tab[:, 1, :, 0:1], 0.0).then_inc(pool_step, 1)
                pool.wait_ge(pool_step, pool_steps.next())
                for k in range(8):
                    n = 1 << k
                    pc, ps = (bc(s5_pow[:, r, k, QT * q:QT * (q + 1)], [P, QT, n]) for r in range(2))
                    c0, s0 = tab[:, 0, :, 0:n], tab[:, 1, :, 0:n]
                    c1, s1 = tab[:, 0, :, n:2 * n], tab[:, 1, :, n:2 * n]
                    x0, x1 = s5_pt[:, 0, :, 0:n], s5_pt[:, 1, :, 0:n]
                    g.tensor_tensor(c1, c0, pc, ALU.mult).then_inc(pool_step, 1)
                    pool.wait_ge(pool_step, pool_steps.next())
                    g.tensor_tensor(x0, s0, ps, ALU.mult).then_inc(pool_step, 1)
                    pool.wait_ge(pool_step, pool_steps.next())
                    g.tensor_tensor(s1, s0, pc, ALU.mult).then_inc(pool_step, 1)
                    pool.wait_ge(pool_step, pool_steps.next())
                    g.tensor_tensor(x1, c0, ps, ALU.mult).then_inc(pool_step, 1)
                    pool.wait_ge(pool_step, pool_steps.next())
                    g.tensor_tensor(c1, c1, x0, ALU.subtract).then_inc(pool_step, 1)
                    pool.wait_ge(pool_step, pool_steps.next())
                    last = g.tensor_tensor(s1, s1, x1, ALU.add)
                    if k < 7:
                        last.then_inc(pool_step, 1)
                        pool.wait_ge(pool_step, pool_steps.next())
                last.then_inc(sem("s5_table"), 1)
                pool.wait_ge(sem("s5_table"), done("s5_table"))

        def s5_dve(dve):
            v = dve
            dve.wait_ge(sem("s5_landed"), 16 * 5)
            dt, th_, n_, r_, tmp = (s5[k] for k in ("dt", "th", "n", "r", "tmp"))
            l2 = s5_ldt[:, :].rearrange("p (j g) -> p j g", g=2)
            v.tensor_copy(dt[0:64, :], l2[0:64, :, 0]).then_inc(dve_step, 1)
            dve.wait_ge(dve_step, dve_steps.next())
            v.tensor_copy(dt[64:P, :], l2[64:P, :, 1]).then_inc(sem("s5_ldt"), 1)
            dve.wait_ge(sem("s5_ldt"), done("s5_ldt"))
            ev = ident[:, :].rearrange("p (a b c) -> p a b c", b=2, c=S5_C)
            for b in range(2):
                v.tensor_reduce(s5_parity[:, b:b + 1], ev[:, :, b, :], AX.XY, ALU.add).then_inc(dve_step, 1)
                dve.wait_ge(dve_step, dve_steps.next())
            dve.wait_ge(sem("s5_dt"), 1)
            v.tensor_tensor(th_, s5_aim, dt, ALU.mult).then_inc(dve_step, 1)
            dve.wait_ge(dve_step, dve_steps.next())
            v.tensor_scalar(n_, th_, 1.0 / (2 * math.pi), None, ALU.mult).then_inc(dve_step, 1)
            dve.wait_ge(dve_step, dve_steps.next())
            v.tensor_scalar(n_, n_, MAGIC, None, ALU.add).then_inc(dve_step, 1)
            dve.wait_ge(dve_step, dve_steps.next())
            v.tensor_scalar(n_, n_, MAGIC, None, ALU.subtract).then_inc(dve_step, 1)
            dve.wait_ge(dve_step, dve_steps.next())
            src = th_
            for part in TWO_PI:
                v.scalar_tensor_tensor(out=r_, in0=n_, scalar=-part, in1=src, op0=ALU.mult, op1=ALU.add).then_inc(dve_step, 1)
                dve.wait_ge(dve_step, dve_steps.next())
                src = r_
            v.tensor_scalar(r_, r_, PI_BELOW, -PI_BELOW, ALU.min, ALU.max).then_inc(dve_step, 1)
            dve.wait_ge(dve_step, dve_steps.next())
            v.tensor_tensor(tmp, s5_are, dt, ALU.mult).then_inc(sem("s5_re_dt"), 1)
            dve.wait_ge(sem("s5_re_dt"), done("s5_re_dt"))
            dve.wait_ge(sem("s5_sin"), 1)
            c1, s1 = s5_pow[:, 0, 0, :], s5_pow[:, 1, 0, :]
            v.tensor_tensor(c1, s5["half"], s5["half"], ALU.mult).then_inc(dve_step, 1)
            dve.wait_ge(dve_step, dve_steps.next())
            v.tensor_scalar(c1, c1, -2.0, 1.0, ALU.mult, ALU.add).then_inc(dve_step, 1)
            dve.wait_ge(dve_step, dve_steps.next())
            v.tensor_copy(s1, s5["sin"]).then_inc(dve_step, 1)
            dve.wait_ge(dve_step, dve_steps.next())
            for k in range(7):
                c, s = s5_pow[:, 0, k, :], s5_pow[:, 1, k, :]
                c2, s2 = s5_pow[:, 0, k + 1, :], s5_pow[:, 1, k + 1, :]
                v.tensor_tensor(c2, c, c, ALU.mult).then_inc(dve_step, 1)
                dve.wait_ge(dve_step, dve_steps.next())
                v.tensor_tensor(n_, s, s, ALU.mult).then_inc(dve_step, 1)
                dve.wait_ge(dve_step, dve_steps.next())
                v.tensor_tensor(c2, c2, n_, ALU.subtract).then_inc(dve_step, 1)
                dve.wait_ge(dve_step, dve_steps.next())
                v.tensor_tensor(s2, c, s, ALU.mult).then_inc(dve_step, 1)
                dve.wait_ge(dve_step, dve_steps.next())
                last = v.tensor_scalar(s2, s2, 2.0, None, ALU.mult)
                if k < 6:
                    last.then_inc(dve_step, 1)
                    dve.wait_ge(dve_step, dve_steps.next())
            last.then_inc(sem("s5_pow"), 1)
            dve.wait_ge(sem("s5_pow"), done("s5_pow"))
            nr, ni, den, cr, ci = (s5[k] for k in ("nr", "r", "den", "cr", "ci"))
            v.tensor_tensor(nr, s5["mag"], c1, ALU.mult).then_inc(dve_step, 1)
            dve.wait_ge(dve_step, dve_steps.next())
            v.tensor_scalar(nr, nr, -1.0, None, ALU.add).then_inc(dve_step, 1)
            dve.wait_ge(dve_step, dve_steps.next())
            v.tensor_tensor(ni, s5["mag"], s1, ALU.mult).then_inc(dve_step, 1)
            dve.wait_ge(dve_step, dve_steps.next())
            v.tensor_tensor(den, s5_are, s5_are, ALU.mult).then_inc(dve_step, 1)
            dve.wait_ge(dve_step, dve_steps.next())
            v.tensor_tensor(tmp, s5_aim, s5_aim, ALU.mult).then_inc(dve_step, 1)
            dve.wait_ge(dve_step, dve_steps.next())
            v.tensor_tensor(den, den, tmp, ALU.add).then_inc(dve_step, 1)
            dve.wait_ge(dve_step, dve_steps.next())
            v.reciprocal(den, den).then_inc(dve_step, 1)
            dve.wait_ge(dve_step, dve_steps.next())
            for dst, x, y, op in ((cr, nr, ni, ALU.add), (ci, ni, nr, ALU.subtract)):
                v.tensor_tensor(dst, x, s5_are, ALU.mult).then_inc(dve_step, 1)
                dve.wait_ge(dve_step, dve_steps.next())
                v.tensor_tensor(tmp, y, s5_aim, ALU.mult).then_inc(dve_step, 1)
                dve.wait_ge(dve_step, dve_steps.next())
                v.tensor_tensor(dst, dst, tmp, op).then_inc(dve_step, 1)
                dve.wait_ge(dve_step, dve_steps.next())
                v.tensor_tensor(dst, dst, den, ALU.mult).then_inc(dve_step, 1)
                dve.wait_ge(dve_step, dve_steps.next())
            v.memset(scr(3), 0.0).then_inc(dve_step, 1)
            dve.wait_ge(dve_step, dve_steps.next())
            for b in range(2):
                ps = slice(64 * b, 64 * b + 64)
                sh = [64, S5_TILES, S5_C]
                for r, (x, y, op) in enumerate(((cr, ci, ALU.subtract), (ci, cr, ALU.add))):
                    v.tensor_tensor(s5_t[ps, 0, :, :], s5_braw[ps, 0, :, :], bc(x[ps, :], sh), ALU.mult).then_inc(dve_step, 1)
                    dve.wait_ge(dve_step, dve_steps.next())
                    v.tensor_tensor(s5_t[ps, 1, :, :], s5_braw[ps, 1, :, :], bc(y[ps, :], sh), ALU.mult).then_inc(dve_step, 1)
                    dve.wait_ge(dve_step, dve_steps.next())
                    last = v.tensor_tensor(s5_bst[ps, r, :, b, :], s5_t[ps, 0, :, :], s5_t[ps, 1, :, :], op)
                    if (b, r) != (1, 1):
                        last.then_inc(dve_step, 1)
                        dve.wait_ge(dve_step, dve_steps.next())
            last.then_inc(sem("s5_bT"), 1)
            dve.wait_ge(sem("s5_bT"), done("s5_bT"))
            for r in range(2):
                for b in range(2):
                    last = v.tensor_scalar(s5_cst[:, r, :, 64 * b:64 * b + 64], s5_craw[:, r, :, :], s5_parity[:, b:b + 1],
                                           1.0 if r == 0 else -1.0, ALU.mult, ALU.mult)
                    if (r, b) != (1, 1):
                        last.then_inc(dve_step, 1)
                        dve.wait_ge(dve_step, dve_steps.next())
            last.then_inc(sem("s5_cT"), 1)
            dve.wait_ge(sem("s5_cT"), done("s5_cT"))

            def y_of(q):
                dve.wait_ge(psum_ready, job("s5", "y", q))
                bank = bank_of("s5", "y", q)
                x = slice(T * q, T * (q + 1))
                v.scalar_tensor_tensor(out=s5_y[:, x], in0=s5_u[:, x], scalar=s5_d[:, q:q + 1], in1=bank[:, 0:T],
                                                 op0=ALU.mult, op1=ALU.add).then_inc(dve_took, 1)
                dve.wait_ge(dve_took, dve_reads.next())

            for q in range(KT):
                tab, w, g, x = s5_tab[q % 2], s5_w, s5_g, s5_x[q % 2]
                dve.wait_ge(sem("s5_table"), q + 1)
                if q >= 2:
                    dve.wait_ge(psum_ready, job("s5", "y", q - 2))
                for j in range(QT):
                    dve.wait_ge(psum_ready, job("s5", "bu", QT * q + j))
                    bank = bank_of("s5", "bu", QT * q + j)
                    re, im = bank[:, 0:T], bank[:, T:2 * T]
                    c, s = tab[:, 0, j, :], tab[:, 1, j, :]
                    v.tensor_tensor(w[:, 0, j, :], re, c, ALU.mult).then_inc(dve_step, 1)
                    dve.wait_ge(dve_step, dve_steps.next())
                    v.tensor_tensor(g[:, 0, j, :], im, s, ALU.mult).then_inc(dve_step, 1)
                    dve.wait_ge(dve_step, dve_steps.next())
                    v.tensor_tensor(w[:, 1, j, :], im, c, ALU.mult).then_inc(dve_step, 1)
                    dve.wait_ge(dve_step, dve_steps.next())
                    v.tensor_tensor(g[:, 1, j, :], re, s, ALU.mult).then_inc(dve_took, 1)
                    dve.wait_ge(dve_took, dve_reads.next())
                    v.tensor_tensor(w[:, 0, j, :], w[:, 0, j, :], g[:, 0, j, :], ALU.add).then_inc(dve_step, 1)
                    dve.wait_ge(dve_step, dve_steps.next())
                    v.tensor_tensor(w[:, 1, j, :], w[:, 1, j, :], g[:, 1, j, :], ALU.subtract).then_inc(dve_step, 1)
                    dve.wait_ge(dve_step, dve_steps.next())
                    mag = s5["mag"][:, QT * q + j:QT * q + j + 1].broadcast_to([P, T])
                    for r in range(2):
                        v.tensor_tensor_scan(g[:, r, j, :], mag, w[:, r, j, :], 0.0, ALU.mult, ALU.add).then_inc(dve_step, 1)
                        dve.wait_ge(dve_step, dve_steps.next())
                c, s = tab[:, 0, :, :], tab[:, 1, :, :]
                v.tensor_tensor(x[:, 0, :, :], g[:, 0, :, :], c, ALU.mult).then_inc(dve_step, 1)
                dve.wait_ge(dve_step, dve_steps.next())
                v.tensor_tensor(w[:, 0, :, :], g[:, 1, :, :], s, ALU.mult).then_inc(dve_step, 1)
                dve.wait_ge(dve_step, dve_steps.next())
                v.tensor_tensor(x[:, 1, :, :], g[:, 0, :, :], s, ALU.mult).then_inc(dve_step, 1)
                dve.wait_ge(dve_step, dve_steps.next())
                v.tensor_tensor(w[:, 1, :, :], g[:, 1, :, :], c, ALU.mult).then_inc(dve_step, 1)
                dve.wait_ge(dve_step, dve_steps.next())
                v.tensor_tensor(x[:, 0, :, :], x[:, 0, :, :], w[:, 0, :, :], ALU.subtract).then_inc(dve_step, 1)
                dve.wait_ge(dve_step, dve_steps.next())
                v.tensor_tensor(x[:, 1, :, :], x[:, 1, :, :], w[:, 1, :, :], ALU.add).then_inc(sem("s5_x"), 1)
                dve.wait_ge(sem("s5_x"), done("s5_x"))
                if q >= 1:
                    y_of(q - 1)
            y_of(KT - 1)

        def s5_mix_dve(dve, total):
            dve.wait_ge(sem(OUT_UNIT), total)
            dve.wait_ge(*taken("s5", "zb", 3))
            for t in range(TT):
                dve.tensor_tensor(s5_mix[:, t, :], acc[:, t, :], s5_sg[:, t, :], ALU.mult).then_inc(dve_step, 1)
                dve.wait_ge(dve_step, dve_steps.next())

        first_w = W["a_w_in"][0]
        plan = {}

        def plan_out(stage, w, n=4):
            plan[stage] = add_out(w, n)

        declare_turn(0)
        declare_dn()
        plan["dn_in"] = add_projection("dn", "qkv", first_w, 0, 12)
        add_projection("dn", "z", first_w, 3 * D, 4)
        plan_out("dn_out", W["a_w_out"][0])
        declare_turn(1)
        declare_route(0)
        moe = [None, None]
        moe[0] = Glu(N_EXP * FF_E // COLS, moe_src(0), True)
        declare_turn(2)
        declare_da()
        plan["da_in"] = add_projection("da", "q", W["b_w_q"][0], 0, 4)
        add_projection("da", "k", W["kv_w"], 0, 4)
        add_projection("da", "v", W["kv_w"], D, 4)
        plan_out("da_out", W["b_w_out"][0])
        declare_turn(3)
        declare_route(1)
        moe[1] = Glu(N_EXP * FF_E // COLS, moe_src(1), True)
        ffn = [None] * 4

        def plan_hg(o):
            declare_turn(HG_LN[o])
            declare_hg(o)
            w = W["hgrn_w_in_2"][o]
            plan[f"hg{o}_in"] = add_projection(f"hg{o}", "f", w, D, 4)
            add_projection(f"hg{o}", "q", w, 0, 4)
            add_projection(f"hg{o}", "g", w, 3 * D, 4)
            add_projection(f"hg{o}", "v", w, 2 * D, 4)
            plan_out(f"hg{o}_out", W["hgrn_w_out_2"][o])

        def plan_ffn(n, turn):
            declare_turn(turn)
            ffn[n] = Glu(FF // COLS, ffn_src(n), False)

        plan_hg(0)
        plan_ffn(0, 5)
        declare_turn(ML_TURN)
        declare_ml()
        w = W["mlstm_w_in_2"][0]
        plan["ml_in"] = add_projection("ml", "qk", w, 0, 4)
        add_projection("ml", "og", w, 2 * D, 4)
        add_projection("ml", "v", w, D, 4)
        plan_out("ml_out", W["mlstm_w_out_2"][0])
        plan_ffn(1, 7)
        declare_turn(S5_TURN)
        declare_s5()
        plan["s5_in"] = add_projection("s5", "u", W["s5_w_in_2"][0], 0, 4)
        plan_out("s5_out", W["s5_w_out_2"][0])
        plan["s5_zb"] = add_projection("s5", "zb", W["s5_w_out_2"][0], D, 4)
        plan_ffn(2, 9)
        plan_hg(1)
        plan_ffn(3, 11)

        def wait_out(stage):
            return lambda eng: eng.wait_ge(sem(OUT_UNIT), plan[stage][1])

        block = ctx.enter_context(nc.Block())

        @block.sync
        def _(sp):
            sp.dma_start(h[:, :, :], W["x"][0].rearrange("(t p) d -> p t d", p=P)).then_inc(sem("x_landed"), 16)
            sp_loads(sp)
            sp.wait_ge(sem("ln_done"), 2 * N_LN)
            sp.dma_start(out[0].rearrange("(t p) d -> p t d", p=P), h[:, :, :]).then_inc(sem("out_stored"), 16)
            sp.wait_ge(sem("out_stored"), 16)

        @block.gpsimd
        def _(pool):
            setup_pool(pool)
            norms = [(W[f"ln_{k}_g"][n], W[f"ln_{k}_b"][n]) for n in range(2) for k in ("mix", "ffn")]
            norms += [(W["ln_g_2"][n, k], W["ln_b_2"][n, k]) for n in range(4) for k in range(2)]
            for n, (g, b) in enumerate(norms):
                if n == HG_LN[0]:
                    hg_pool(pool, 0)
                if n == ML_TURN:
                    ml_pool(pool)
                if n == S5_TURN:
                    s5_pool(pool)
                if n == HG_LN[1]:
                    hg_pool(pool, 1)
                ln_params(pool, n, g, b)

        @block.tensor
        def _(pe):

            def out_of(stage, src, key, n=4):
                for i in range(4):
                    pe.wait_ge(*taken(key, "oT", i))
                project_out(pe, plan[stage][0], n, src)

            def swiglu(turn, g):
                wait_turned(pe, turn)
                glu_pe(pe, g)

            setup_pe(pe)
            turn_pe(pe, 0)
            dn_pe(pe, plan["dn_in"])
            out_of("dn_out", dn_oT, "dn")
            turn_pe(pe, 1)
            route_pe(pe, 0, 1)
            swiglu(1, moe[0])
            turn_pe(pe, 2)
            da_pe(pe, plan["da_in"])
            out_of("da_out", da_oT, "da")
            turn_pe(pe, 3)
            route_pe(pe, 1, 3)
            swiglu(3, moe[1])
            turn_pe(pe, 4)
            hg_pe(pe, 0, plan["hg0_in"])
            out_of("hg0_out", hg_oT, "hg0")
            turn_pe(pe, 5)
            swiglu(5, ffn[0])
            turn_pe(pe, ML_TURN)
            ml_pe(pe, plan["ml_in"])
            out_of("ml_out", ml_oT, "ml")
            turn_pe(pe, 7)
            swiglu(7, ffn[1])
            turn_pe(pe, S5_TURN)
            s5_pe(pe, plan["s5_in"])
            project_out(pe, plan["s5_out"][0], 4, s5_oT)
            project_tokens(pe, "s5", "zb", 4, plan["s5_zb"], s5_oT)
            turn_pe(pe, 9)
            swiglu(9, ffn[2])
            turn_pe(pe, HG_LN[1])
            hg_pe(pe, 1, plan["hg1_in"])
            out_of("hg1_out", hg_oT, "hg1")
            turn_pe(pe, 11)
            swiglu(11, ffn[3])

        @block.scalar
        def _(act):

            def norm(n):
                ln_act(act, n)
                if n + 1 < N_LN:
                    turn_act(act, n + 1)

            turn_act(act, 0)
            dn_act(act)
            norm(0)
            route_act(act, 0)
            glu_steps_of(act, moe[0], glu_silu)
            norm(1)
            da_act(act)
            norm(2)
            route_act(act, 1)
            glu_steps_of(act, moe[1], glu_silu)
            norm(3)
            hg_act(act, 0)
            norm(4)
            glu_steps_of(act, ffn[0], glu_silu)
            norm(5)
            ml_act(act)
            norm(6)
            glu_steps_of(act, ffn[1], glu_silu)
            norm(7)
            s5_act(act)
            norm(8)
            glu_steps_of(act, ffn[2], glu_silu)
            norm(9)
            hg_act(act, 1)
            norm(10)
            glu_steps_of(act, ffn[3], glu_silu)
            norm(11)

        @block.vector
        def _(dve):
            dn_dve(dve)
            ln_dve(dve, 0, ALPHA_FIRST, wait_out("dn_out"))
            route_dve(dve, 0)
            glu_steps_of(dve, moe[0], glu_hid)
            ln_dve(dve, 1, ALPHA_FIRST, wait_glu(moe[0]))
            da_dve(dve)
            ln_dve(dve, 2, ALPHA_FIRST, wait_out("da_out"))
            route_dve(dve, 1)
            glu_steps_of(dve, moe[1], glu_hid)
            ln_dve(dve, 3, ALPHA_FIRST, wait_glu(moe[1]))
            hg_dve(dve, 0)
            ln_dve(dve, 4, ALPHA_SECOND, wait_out("hg0_out"))
            glu_steps_of(dve, ffn[0], glu_hid)
            ln_dve(dve, 5, ALPHA_SECOND, wait_glu(ffn[0]))
            ml_dve(dve)
            ln_dve(dve, 6, ALPHA_SECOND, wait_out("ml_out"))
            glu_steps_of(dve, ffn[1], glu_hid)
            ln_dve(dve, 7, ALPHA_SECOND, wait_glu(ffn[1]))
            s5_dve(dve)
            s5_mix_dve(dve, plan["s5_out"][1])
            ln_dve(dve, 8, ALPHA_SECOND, lambda eng: None, s5_mix)
            glu_steps_of(dve, ffn[2], glu_hid)
            ln_dve(dve, 9, ALPHA_SECOND, wait_glu(ffn[2]))
            hg_dve(dve, 1)
            ln_dve(dve, 10, ALPHA_SECOND, wait_out("hg1_out"))
            glu_steps_of(dve, ffn[3], glu_hid)
            ln_dve(dve, 11, ALPHA_SECOND, wait_glu(ffn[3]))


def kernel(**inputs):
    from concourse import bacc
    from concourse.bass_utils import run_bass_kernel_spmd

    nc = bacc.Bacc("TRN2", target_bir_lowering=False, num_devices=1)
    arrays, params = {}, {}
    for name, value in inputs.items():
        a = np.ascontiguousarray(value)
        arrays[name] = a
        params[name] = nc.dram_tensor(name, a.shape, mybir.dt.from_np(a.dtype), kind="ExternalInput").ap()
    out = nc.dram_tensor("out", arrays["x"].shape, F32, kind="ExternalOutput").ap()
    build(nc, params, out)
    r = run_bass_kernel_spmd(nc, [arrays], core_ids=[0])
    return r.results[0]["out"]
```
